# Optimizing a Trainium2 kernel written in Bass

```python
import math
import jax, jax.numpy as jnp
from jax import lax
import numpy as np

D_MODEL = 1024
BATCH = 1
SEQ = 512
DEPTH = 2

CHUNK = 64
Q_BLOCK = 128
N_MIXERS = 2
N_CONV_LAYERS = (DEPTH + 1) // 2
N_ATTN_LAYERS = DEPTH // 2
CONV_WIDTH = 31
N_HEADS = 8
HEAD_DIM = D_MODEL // N_HEADS // 2
V_DIM = 2 * HEAD_DIM
N_GROUPS = 4
EXPERTS_PER_GROUP = 8
N_EXPERTS = N_GROUPS * EXPERTS_PER_GROUP
TOP_K = 2
D_EXPERT = D_MODEL // 2
ROW_BLOCK = 256
EPS = 1e-6

kernel_name = "hybrid_conv_diffattn_hmoe"

def rms_norm(x, g):
    xf = x.astype(jnp.float32)
    y = xf * lax.rsqrt(jnp.mean(xf * xf, axis=-1, keepdims=True) + EPS)
    return (y * g.astype(jnp.float32)).astype(x.dtype)

def layer_norm(x, g, b):
    xf = x.astype(jnp.float32)
    mu = jnp.mean(xf, axis=-1, keepdims=True)
    var = jnp.mean(jnp.square(xf - mu), axis=-1, keepdims=True)
    y = (xf - mu) * lax.rsqrt(var + EPS)
    return (y * g.astype(jnp.float32) + b.astype(jnp.float32)).astype(x.dtype)

def lambda_init_fn(layer_idx):
    return 0.8 - 0.6 * math.exp(-0.3 * layer_idx)

def conformer_conv(h, w_in, b_in, dw, dw_b, ln_g, ln_b, w_out, b_out):
    u = h @ w_in + b_in
    a, g = jnp.split(u, 2, axis=-1)
    u = a * jax.nn.sigmoid(g)
    u = lax.conv_general_dilated(
        u, dw[:, None, :].astype(u.dtype), window_strides=(1,),
        padding=[(CONV_WIDTH - 1, 0)],
        dimension_numbers=("NWC", "WIO", "NWC"),
        feature_group_count=D_MODEL) + dw_b
    u = jax.nn.silu(layer_norm(u, ln_g, ln_b))
    return u @ w_out + b_out

def diff_attention(h, w_qkv, q_g, k_g, lq1, lk1, lq2, lk2, subln_g, w_o, lambda_init):
    B, S, _ = h.shape
    qkv = h @ w_qkv
    q, k, v = jnp.split(qkv, 3, axis=-1)
    q = rms_norm(q.reshape(B, S, N_HEADS, 2, HEAD_DIM), q_g) * (HEAD_DIM ** -0.5)
    k = rms_norm(k.reshape(B, S, N_HEADS, 2, HEAD_DIM), k_g)
    q = q.transpose(0, 2, 3, 1, 4)
    k = k.transpose(0, 2, 3, 1, 4)
    v = v.reshape(B, S, N_HEADS, V_DIM).transpose(0, 2, 1, 3)
    lam = (jnp.exp(jnp.sum(lq1.astype(jnp.float32) * lk1.astype(jnp.float32)))
           - jnp.exp(jnp.sum(lq2.astype(jnp.float32) * lk2.astype(jnp.float32)))
           + lambda_init)
    outs = []
    for start in range(0, S, Q_BLOCK):
        end = start + Q_BLOCK
        qb = q[:, :, :, start:end]
        kb = k[:, :, :, :end]
        vb = v[:, :, :end]
        s = jnp.einsum("bhcqd,bhckd->bhcqk", qb, kb).astype(jnp.float32)
        q_chunk = (start + jnp.arange(Q_BLOCK)) // CHUNK
        k_chunk = jnp.arange(end) // CHUNK
        mask = k_chunk[None, :] <= q_chunk[:, None]
        p = jax.nn.softmax(jnp.where(mask, s, -jnp.inf), axis=-1)
        a = p[:, :, 0] - lam * p[:, :, 1]
        outs.append(jnp.einsum("bhqk,bhkd->bhqd", a.astype(vb.dtype), vb))
    o = jnp.concatenate(outs, axis=2)
    o = rms_norm(o, subln_g) * (1.0 - lambda_init)
    o = o.transpose(0, 2, 1, 3).reshape(B, S, D_MODEL)
    return o @ w_o

def hierarchical_moe(h, w_grp, b_grp, w_exp, b_exp, w1, w3, w2):
    B, S, D = h.shape
    T = B * S
    hf = h.reshape(T, D)
    h32 = hf.astype(jnp.float32)
    grp_prob = jax.nn.softmax(h32 @ w_grp.astype(jnp.float32) + b_grp.astype(jnp.float32), axis=-1)
    grp_p, grp_idx = lax.top_k(grp_prob, 1)
    exp_logits = (h32 @ w_exp.astype(jnp.float32) + b_exp.astype(jnp.float32)
                  ).reshape(T, N_GROUPS, EXPERTS_PER_GROUP)
    sel = jnp.take_along_axis(exp_logits, grp_idx[:, :, None], axis=1)[:, 0]
    top_p, top_j = lax.top_k(jax.nn.softmax(sel, axis=-1), TOP_K)
    gates = grp_p * top_p / jnp.sum(top_p, axis=-1, keepdims=True)
    experts = grp_idx * EXPERTS_PER_GROUP + top_j

    A = T * TOP_K
    flat_e = experts.reshape(-1)
    order = jnp.argsort(flat_e)
    e_sorted = flat_e[order]
    tok_sorted = order // TOP_K
    gate_sorted = gates.reshape(-1)[order]
    counts = jnp.bincount(flat_e, length=N_EXPERTS)
    starts = jnp.cumsum(counts) - counts
    padded = (counts + ROW_BLOCK - 1) // ROW_BLOCK * ROW_BLOCK
    pad_ends = jnp.cumsum(padded)
    pad_starts = pad_ends - padded
    dest = pad_starts[e_sorted] + jnp.arange(A) - starts[e_sorted]
    n_blocks = -(-A // ROW_BLOCK) + N_EXPERTS
    row_tok = jnp.zeros((n_blocks * ROW_BLOCK,), jnp.int32).at[dest].set(tok_sorted)
    block_e = jnp.minimum(
        jnp.searchsorted(pad_ends, jnp.arange(n_blocks) * ROW_BLOCK, side="right"),
        N_EXPERTS - 1)
    xb = hf[row_tok].reshape(n_blocks, ROW_BLOCK, D)

    def expert_block(args):
        xr, e = args
        return (jax.nn.silu(xr @ w1[e]) * (xr @ w3[e])) @ w2[e]

    yb = lax.map(expert_block, (xb, block_e)).reshape(n_blocks * ROW_BLOCK, D)
    y_assign = yb[dest] * gate_sorted[:, None].astype(yb.dtype)
    out = jnp.zeros((T, D), dtype=yb.dtype).at[tok_sorted].add(y_assign)
    return out.reshape(B, S, D)

def setup_inputs(seed: int = 0) -> dict:
    key = jax.random.key(seed)
    ks = iter(jax.random.split(key, 32))
    f32 = jnp.float32

    def nrm(shape, scale):
        return jax.random.normal(next(ks), shape, f32) * scale

    def gain(shape):
        return 1.0 + nrm(shape, 0.02)

    D, NC, NA = D_MODEL, N_CONV_LAYERS, N_ATTN_LAYERS
    return {
        "x": nrm((BATCH, SEQ, D), 1.0),
        "norm1_g": gain((DEPTH, D)),
        "norm2_g": gain((DEPTH, D)),
        "conv_w_in": nrm((NC, D, 2 * D), D ** -0.5),
        "conv_b_in": nrm((NC, 2 * D), 0.02),
        "conv_dw": nrm((NC, CONV_WIDTH, D), CONV_WIDTH ** -0.5),
        "conv_dw_b": nrm((NC, D), 0.02),
        "conv_ln_g": gain((NC, D)),
        "conv_ln_b": nrm((NC, D), 0.02),
        "conv_w_out": nrm((NC, D, D), D ** -0.5),
        "conv_b_out": nrm((NC, D), 0.02),
        "attn_w_qkv": nrm((NA, D, 3 * D), D ** -0.5),
        "attn_q_g": gain((NA, HEAD_DIM)),
        "attn_k_g": gain((NA, HEAD_DIM)),
        "attn_lq1": nrm((NA, HEAD_DIM), 0.1),
        "attn_lk1": nrm((NA, HEAD_DIM), 0.1),
        "attn_lq2": nrm((NA, HEAD_DIM), 0.1),
        "attn_lk2": nrm((NA, HEAD_DIM), 0.1),
        "attn_subln_g": gain((NA, V_DIM)),
        "attn_w_o": nrm((NA, D, D), D ** -0.5),
        "moe_w_grp": nrm((DEPTH, D, N_GROUPS), D ** -0.5),
        "moe_b_grp": nrm((DEPTH, N_GROUPS), 0.01),
        "moe_w_exp": nrm((DEPTH, D, N_EXPERTS), D ** -0.5),
        "moe_b_exp": nrm((DEPTH, N_EXPERTS), 0.01),
        "moe_w1": nrm((DEPTH, N_EXPERTS, D, D_EXPERT), D ** -0.5),
        "moe_w3": nrm((DEPTH, N_EXPERTS, D, D_EXPERT), D ** -0.5),
        "moe_w2": nrm((DEPTH, N_EXPERTS, D_EXPERT, D), D_EXPERT ** -0.5),
    }

def reference(x, norm1_g, norm2_g,
              conv_w_in, conv_b_in, conv_dw, conv_dw_b, conv_ln_g, conv_ln_b, conv_w_out, conv_b_out,
              attn_w_qkv, attn_q_g, attn_k_g, attn_lq1, attn_lk1, attn_lq2, attn_lk2, attn_subln_g, attn_w_o,
              moe_w_grp, moe_b_grp, moe_w_exp, moe_b_exp, moe_w1, moe_w3, moe_w2):
    for i in range(DEPTH):
        h = rms_norm(x, norm1_g[i])
        j = i // N_MIXERS
        if i % N_MIXERS == 0:
            mix = conformer_conv(h, conv_w_in[j], conv_b_in[j], conv_dw[j], conv_dw_b[j],
                                 conv_ln_g[j], conv_ln_b[j], conv_w_out[j], conv_b_out[j])
        else:
            mix = diff_attention(h, attn_w_qkv[j], attn_q_g[j], attn_k_g[j],
                                 attn_lq1[j], attn_lk1[j], attn_lq2[j], attn_lk2[j],
                                 attn_subln_g[j], attn_w_o[j], lambda_init_fn(i))
        x = x + mix
        h = rms_norm(x, norm2_g[i])
        x = x + hierarchical_moe(h, moe_w_grp[i], moe_b_grp[i], moe_w_exp[i], moe_b_exp[i],
                                 moe_w1[i], moe_w3[i], moe_w2[i])
    return x


_drawn_inputs = setup_inputs


def setup_inputs(seed=0):
    import zlib

    import numpy as np

    out = dict(_drawn_inputs(seed))
    spreads = {}
    factors = {'attn_q_g': 4.045,
     'attn_k_g': 3.078,
     'attn_lq1': 5.234,
     'attn_subln_g': 2.832,
     'moe_b_grp': 8.0,
     'moe_b_exp': 3.95}
    for name, (base, spread) in spreads.items():
        noise = np.random.default_rng([zlib.crc32(name.encode()), seed]).standard_normal(out[name].shape)
        drawn = base * np.exp(spread * noise) if base else spread * noise
        out[name] = __import__('jax').numpy.asarray(drawn.astype(out[name].dtype))
    for name, factor in factors.items():
        out[name] = (out[name] * factor).astype(out[name].dtype)
    return out
```

```python
import math
from contextlib import ExitStack

import concourse.bass as bass
from concourse import mybir

F32 = mybir.dt.float32
F16 = mybir.dt.float16
BF16 = mybir.dt.bfloat16
I32 = mybir.dt.int32
ALU = mybir.AluOpType
ACT = mybir.ActivationFunctionType
AX = mybir.AxisListType

P = 128
D = 1024
T = 512
NT = T // P
NC = D // P
EPS = 1e-6
TAPS = 31
POOL_TAPS = 11
HEADS = 8
HEAD_DIM = 64
CHUNK = 64
GROUPS = 4
PER_GROUP = 8
EXPERTS = GROUPS * PER_GROUP
D_EXPERT = 512
ROUTES = GROUPS + EXPERTS
SLOTS = 64
ASSIGN = 2 * T
OVER = (ASSIGN - 1) // (SLOTS + 1)
TILES = EXPERTS + OVER
STEPS = T // SLOTS - 1
RING = 6
UNIT = 4096
BIG = 3.0e38
FAR = 1.0e6
LAYERS = 2
MIX_UNITS = (6, 8)
MOE_UNITS = 3 * EXPERTS
FIRST = (0, MIX_UNITS[0] + MOE_UNITS)
ROUTE_LOADS = 16 * (9 + 6 * LAYERS)
LAMBDA_INIT = 0.8 - 0.6 * math.exp(-0.3 * 1)


def trunk(nc, x, norm1_g, norm2_g, conv_w_in, conv_b_in, conv_dw, conv_dw_b, conv_ln_g, conv_ln_b,
          conv_w_out, conv_b_out, attn_w_qkv, attn_q_g, attn_k_g, attn_lq1, attn_lk1, attn_lq2,
          attn_lk2, attn_subln_g, attn_w_o, moe_w_grp, moe_b_grp, moe_w_exp, moe_b_exp, moe_w1,
          moe_w3, moe_w2, out):
    ctx = ExitStack()

    def sb(name, shape, dt=F32):
        return ctx.enter_context(nc.sbuf_tensor(name, shape, dt))

    def sem(name):
        return ctx.enter_context(nc.semaphore(name))

    with ctx:
        x_res = sb("x_res", [P, NT, D])
        hT = sb("hT", [P, NC, T])
        ring = sb("ring", [P, RING, UNIT])
        area1 = sb("area1", [P, UNIT])
        area2 = sb("area2", [P, UNIT])
        area3 = sb("area3", [P, UNIT])
        scratch = sb("scratch", [P, 5632])
        ident = sb("ident", [P, P])
        ones = sb("ones", [P, P])
        halves = sb("halves", [P, P])
        iota_slot = sb("iota_slot", [P, P])
        iota_tile = sb("iota_tile", [P, TILES])
        iota_exp = sb("iota_exp", [P, EXPERTS])
        steps = sb("steps", [P, STEPS])
        step_count = sb("step_count", [P, 2 * NT])
        assign1 = sb("assign1", [P, 2, NT])
        half_m2 = sb("half_m2", [P, 1])
        eps = sb("eps", [P, 1])
        mask_row = sb("mask_row", [1, P], BF16)
        mask_col = sb("mask_col", [1, CHUNK], BF16)
        ones16 = sb("ones16", [P, P], F16)
        before16 = sb("before16", [P, P], F16)
        norm_g = sb("norm_g", [P, 2 * LAYERS, NC])
        w_route = sb("w_route", [P, LAYERS, NC, ROUTES])
        b_route = sb("b_route", [1, LAYERS, ROUTES])
        chan = sb("chan", [P, NC, TAPS + 5])
        qk_g = sb("qk_g", [P, 2])
        sub_g = sb("sub_g", [P, 1])
        lam_in = sb("lam_in", [P, 4, HEAD_DIM])
        small = sb("small", [P, 64])
        gates = sb("gates", [P, 2, NT])
        gain_sb = sb("gain_sb", [P, LAYERS, NC])
        ctl = sb("ctl", [1, 1 + OVER], I32)
        rows_in = sb("rows_in", [P, TILES], I32)
        rows_out = sb("rows_out", [P, TILES], I32)
        at_in = sb("at_in", [P, 2], I32)
        at_out = sb("at_out", [P, 2], I32)
        banks2 = [ctx.enter_context(nc.psum_tensor(f"banks{2 * i}_{2 * i + 1}", [P, 2, 512], F32)) for i in range(4)]
        bank = [banks2[i // 2][:, i % 2, :] for i in range(8)]

        xn_dram = [nc.dram_tensor(f"xn_dram{l}", [2 * T, D // 2], F32, kind="Internal").ap() for l in range(LAYERS)]
        y_dram = [nc.dram_tensor(f"y_dram{l}", [2 * ASSIGN, D // 2], F32, kind="Internal").ap() for l in range(LAYERS)]

        def small_at(a, n=1):
            return small[:, a:a + n]

        ssq, std, rstd = small_at(0, NT), small_at(4, NT), small_at(8, NT)

        consts_ready, params_loaded, x_loaded = sem("consts_ready"), sem("params_loaded"), sem("x_loaded")
        route_loaded = sem("route_loaded")
        unit_loaded = [sem(f"unit_loaded{i}") for i in range(RING)]
        dve_chain, dve_taps = sem("dve_chain"), sem("dve_taps")
        act_chain = sem("act_chain")
        pool_chain = sem("pool_chain")
        ssq_done, std_done, xn_done = sem("ssq_done"), sem("std_done"), sem("xn_done")
        xt_ready, xt_taken = sem("xt_ready"), sem("xt_taken")
        x_done = sem("x_done")
        chan_ready, chan_taken = sem("chan_ready"), sem("chan_taken")
        glu_ready, gate_done, u_done = sem("glu_ready"), sem("gate_done"), sem("u_done")
        tap_made, tap_added, conv_done, sq_done = sem("tap_made"), sem("tap_added"), sem("conv_done"), sem("sq_done")
        stats_ready, ln_var, ln_std, ln_x, ln_done = sem("stats_ready"), sem("ln_var"), sem("ln_std"), sem("ln_x"), sem("ln_done")
        mix_ready = sem("mix_ready")
        xn_stored, logits_ready, exp_in, exp_done = sem("xn_stored"), sem("logits_ready"), sem("exp_in"), sem("exp_done")
        picks_done, ranks_ready, hot_done, lists_ready, lists_done = (
            sem("picks_done"), sem("ranks_ready"), sem("hot_done"), sem("lists_ready"), sem("lists_done"))
        qk_ready, qk_sq, qk_ss, qk_std, qk_done = sem("qk_ready"), sem("qk_sq"), sem("qk_ss"), sem("qk_std"), sem("qk_done")
        v_ready, v_done = sem("v_ready"), sem("v_done")
        s_ready, m_done, p_done, a_done = sem("s_ready"), sem("m_done"), sem("p_done"), sem("a_done")
        aT_ready, aT_done, o_ready, o_done, o_sq = sem("aT_ready"), sem("aT_done"), sem("o_ready"), sem("o_done"), sem("o_sq")
        on_std, on_done, oT_ready, oT_done = sem("on_std"), sem("on_done"), sem("oT_ready"), sem("oT_done")
        lam_sum, lam_exp = sem("lam_sum"), sem("lam_exp")
        names = ("xT_ready", "xT_taken", "up_ready", "silu_done", "h_done", "hid_ready", "hid_taken", "y_ready", "y_taken")
        main = [{n: sem(f"{n}_main{l}") for n in names} for l in range(LAYERS)]
        over = [{n: sem(f"{n}_over{l}") for n in names} for l in range(LAYERS)]
        xe_loaded = [[sem(f"xe_loaded{l}_{s}") for s in range(2)] for l in range(LAYERS)]
        y_stored = [[sem(f"y_stored{l}_{s}") for s in range(2)] for l in range(LAYERS)]
        over_xe = [sem(f"over_xe{l}") for l in range(LAYERS)]
        over_y = [sem(f"over_y{l}") for l in range(LAYERS)]
        over_w = [sem(f"over_w{l}") for l in range(LAYERS)]
        over_w2 = [sem(f"over_w2{l}") for l in range(LAYERS)]
        at_copied = [sem(f"at_copied{l}") for l in range(LAYERS)]
        at_copied_over = [sem(f"at_copied_over{l}") for l in range(LAYERS)]
        moe_over = sem("moe_over")
        waits_alone = sem("waits_alone")
        y_loaded = [sem(f"y_loaded{t}") for t in range(NT)]
        out_stored = sem("out_stored")

        def alone(eng):
            eng.sem_inc(waits_alone, 1)

        block = ctx.enter_context(nc.Block())

        def unit(n):
            return ring[:, n % RING, :]

        def loaded(eng, n):
            eng.wait_ge(unit_loaded[n % RING], 32 * (n // RING + 1))

        def cols_dram(w, c0, width=512):
            v = w[:, c0:c0 + width].rearrange("(h p j) n -> h p j n", h=2, j=4)
            return [v[h] for h in range(2)]

        def rows_dram(w, c0, width=512):
            v = w[:, c0:c0 + width].rearrange("(h c p) n -> h p c n", h=2, p=P)
            return [v[h] for h in range(2)]

        def w_chunks(n):
            return unit(n).rearrange("p (c n) -> p c n", c=NC)

        xn = area1[:].rearrange("p (t f) -> p t f", t=NT)
        sq_ct = area1[:].rearrange("p (c t) -> p c t", c=NC)
        uT = area2[:].rearrange("p (c t) -> p c t", c=NC)
        chan_rows = area3[0:TAPS + 5, 0:D]
        b_out = area3[0:1, 3072:3072 + D]
        PAD = TAPS - 1
        u_buf = [scratch[:, b * (T + PAD):(b + 1) * (T + PAD)] for b in range(2)]
        base = 2 * (T + PAD)
        sg = [scratch[:, base + b * T:base + (b + 1) * T] for b in range(2)]
        tap = [scratch[:, base + (2 + b) * T:base + (3 + b) * T] for b in range(2)]
        pacc = scratch[:, base + 4 * T:base + 5 * T]
        acc2 = scratch[:, base + 5 * T:base + 6 * T]
        ln_mu = area3[:, 1024:1024 + T]
        ln_r = area3[:, 1024 + T:1024 + 2 * T]
        ln_t = area3[:, 1024 + 2 * T:1024 + 3 * T]
        xe = [scratch[:, s * 512:(s + 1) * 512] for s in range(2)]
        xeT = [scratch[:, 1024 + s * 512:1536 + s * 512].rearrange("p (j h k) -> p j h k", j=4, h=2) for s in range(2)]
        s_sb = [scratch[:, 2048 + s * 512:2560 + s * 512] for s in range(2)]
        h_sb = [scratch[0:SLOTS, 3072 + s * 512:3584 + s * 512] for s in range(2)]
        hidT = [scratch[:, 4096 + s * 256:4352 + s * 256].rearrange("p (j k) -> p j k", j=4) for s in range(2)]
        y_sb = [scratch[:, 4608 + s * 512:5120 + s * 512] for s in range(2)]
        r2 = lambda a, n: area2[:, a:a + n]
        lg = r2(0, NT * ROUTES).rearrange("p (t r) -> p t r", t=NT)
        sel = r2(256, NT * EXPERTS).rearrange("p (t e) -> p t e", t=NT)
        tmp = r2(384, NT * EXPERTS).rearrange("p (t e) -> p t e", t=NT)
        pick = [r2(512 + 128 * k, 128).rearrange("p (t e) -> p t e", t=NT) for k in range(2)]
        both = r2(768, 64).bitcast(F16).rearrange("p (t e) -> p t e", t=NT)
        rank = r2(896, 128).rearrange("p (t e) -> p t e", t=NT)
        count = r2(1024, EXPERTS)
        tiles_e = r2(1056, EXPERTS)
        tiles_inc = r2(1088, EXPERTS)
        tiles_base = r2(1120, EXPERTS)
        cmp = r2(1152, EXPERTS * STEPS)
        g_eq = r2(1376, NT * GROUPS).rearrange("p (t g) -> p t g", t=NT)
        g_cand = r2(1392, NT * GROUPS).rearrange("p (t g) -> p t g", t=NT)
        g_dif = r2(1408, NT * GROUPS).rearrange("p (t g) -> p t g", t=NT)
        g_exp = r2(1424, NT * GROUPS).rearrange("p (t g) -> p t g", t=NT)
        v4 = lambda k: r2(1440 + NT * k, NT)
        v8 = lambda k: r2(1504 + 2 * NT * k, 2 * NT)
        over_cmp = r2(1600, OVER * EXPERTS)
        over_e = r2(2080, OVER + 1)
        list_f = r2(2100, TILES)
        list_pad = r2(2150, TILES)
        list_i = r2(2200, TILES).bitcast(I32)
        list_j = r2(2250, TILES).bitcast(I32)
        hot_slot = area3[:, 0:NT * P].bitcast(F16).rearrange("p (k s) -> p k s", k=2 * NT)
        hot_tile = area3[:, 1024:1024 + NT * TILES].bitcast(F16).rearrange("p (k s) -> p k s", k=2 * NT)
        y_in = [(area1, area2)[t // 2][:, (t % 2) * 2048:(t % 2 + 1) * 2048] for t in range(NT)]
        vv = area1[:].rearrange("p (t f) -> p t f", t=NT)
        qT = area2[:].rearrange("p (h t) -> p h t", h=HEADS)
        kT = area3[:].rearrange("p (h t) -> p h t", h=HEADS)
        o_sb = hT[:].rearrange("p c t -> p (c t)").rearrange("p (t f) -> p t f", t=NT)
        oT = area2[:].rearrange("p (h t) -> p h t", h=HEADS)
        p_sb = [scratch[:, b * 1024:(b + 1) * 1024].rearrange("p (c k) -> p c k", c=2) for b in range(3)]
        a_sb = [scratch[:, 3072 + b * 512:3584 + b * 512] for b in range(2)]
        aT = [scratch[:, 4096 + b * 512:4608 + b * 512] for b in range(2)]
        qk_sqb = [scratch[:, b * 512:(b + 1) * 512] for b in range(2)]
        qk_stdb = [scratch[:, 1024 + b * 512:1536 + b * 512] for b in range(2)]
        qk_rsb = [scratch[:, 2048 + b * 512:2560 + b * 512] for b in range(2)]
        junk = scratch[:, 4608:5632]
        pairs = [(h, b) for h in range(HEADS) for b in range(NT)]
        mx = scratch[:, 5120:5120 + 64].rearrange("p (i c) -> p i c", c=2)
        ps = scratch[:, 5184:5184 + 64].rearrange("p (i c) -> p i c", c=2)
        r1c = scratch[:, 5248:5248 + 32]
        o_ssq = scratch[:, 5280:5280 + 32]
        o_std = scratch[:, 5312:5312 + 32]
        o_r = scratch[:, 5344:5344 + 32]
        o_junk = scratch[:, 5376:5376 + P]
        neg_lam = small_at(12)
        lam_t = small_at(13, 4)
        N_PRE = (0, 2)
        N_MOE = (1, 3)

        @block.sync
        def _(sp):
            def load_unit(dst, halves, done):
                for h in range(2):
                    sp.dma_start(dst[h], halves[h]).then_inc(done, 16)

            def chunk_halves(u):
                return [u[:, h * UNIT // 2:(h + 1) * UNIT // 2].rearrange("p (c n) -> p c n", c=4) for h in range(2)]

            def flat_halves(u):
                return [u[:, h * UNIT // 2:(h + 1) * UNIT // 2] for h in range(2)]

            def mix_unit(n, src):
                load_unit(chunk_halves(unit(n)), src, unit_loaded[n % RING])

            def moe_weights(l, freed, meanwhile):
                n0 = FIRST[l] + MIX_UNITS[l]
                w1v = moe_w1[l].rearrange("e (h p j) n -> e h p (j n)", h=2, j=4)
                w3v = moe_w3[l].rearrange("e (h p j) n -> e h p (j n)", h=2, j=4)
                w2v = moe_w2[l].rearrange("e (p h j) n -> e h p (j n)", h=2, j=2)

                def expert_units(e):
                    return [[w[e, h] for h in range(2)] for w in (w1v, w3v, w2v)]

                def load_expert_unit(i, s):
                    src = expert_units(i * 2 + s // 3)[s % 3]
                    load_unit(flat_halves(unit(n0 + s)), src, unit_loaded[(n0 + s) % RING])

                for s in range(6):
                    sp.wait_ge(*freed[s])
                    load_expert_unit(0, s)
                with sp.Fori(1, EXPERTS // 2) as i:
                    for s in range(6):
                        used = main[l]["up_ready" if s % 3 < 2 else "y_ready"]
                        sp.wait_ge(used, i * 2 + (s // 3 - 1))
                        load_expert_unit(i, s)
                sp.wait_ge(lists_done, l + 1)
                n_over = sp.value_load(ctl[0:1, 0:1], min_val=0, max_val=OVER)

                def over_tile(j):
                    e = sp.value_load(ctl[0:1, bass.ds(j + 1, 1)], min_val=0, max_val=EXPERTS - 1)
                    for k, w in enumerate(expert_units(e)):
                        load_unit(flat_halves(unit(n0 + MOE_UNITS + k)), w, over_w[l] if k < 2 else over_w2[l])

                with sp.If(n_over > 0):
                    sp.wait_ge(main[l]["y_ready"], EXPERTS - 1)
                    over_tile(0)
                meanwhile()
                with sp.If(n_over > 1):
                    with sp.Fori(1, n_over) as j:
                        sp.wait_ge(over[l]["y_ready"], j)
                        alone(sp)
                        over_tile(j)

            w_in, w_out = conv_w_in[0], conv_w_out[0]
            for t in range(NT):
                sp.dma_start(x_res[:, t, :], x[0, t * P:(t + 1) * P, :]).then_inc(x_loaded, 16)
            for n, c0 in enumerate((0, D, 512, D + 512)):
                mix_unit(n, cols_dram(w_in, c0))
            for n in range(2):
                mix_unit(4 + n, rows_dram(w_out, n * 512))
            n0 = FIRST[1]
            w_qkv, w_o = attn_w_qkv[0], attn_w_o[0]
            qkv_cols = (0, D, 512, D + 512, 2 * D, 2 * D + 512)
            done = main[0]

            def last_qkv():
                for n in range(3, 6):
                    sp.wait_ge(done["up_ready" if n < 5 else "y_ready"], EXPERTS)
                    mix_unit(n0 + n, cols_dram(w_qkv, qkv_cols[n]))

            moe_weights(0, [(glu_ready, 4)] * 2 + [(glu_ready, 8)] * 2 + [(mix_ready, 8)] * 2, last_qkv)
            sp.wait_ge(moe_over, 1)
            for n in range(3):
                mix_unit(n0 + n, cols_dram(w_qkv, qkv_cols[n]))
            sp.wait_ge(qk_ready, 8)
            for n in range(2):
                mix_unit(n0 + 6 + n, rows_dram(w_o, n * 512))
            moe_weights(1, [(qk_ready, 16)] * 2 + [(v_ready, NT), (v_ready, 2 * NT)] + [(mix_ready, 16)] * 2,
                        lambda: None)
            for t in range(NT):
                sp.wait_ge(x_done, 12 + t + 1)
                sp.dma_start(out[0, t * P:(t + 1) * P, :], x_res[:, t, :]).then_inc(out_stored, 16)
            sp.wait_ge(out_stored, 16 * NT)

        @block.gpsimd
        def _(pool):
            g = nc.gpsimd
            linked = [0]

            def link(ins):
                linked[0] += 1
                ins.then_inc(pool_chain, 1)
                pool.wait_ge(pool_chain, linked[0])

            link(g.memset(ones[:], 1.0))
            link(g.memset(eps[:], EPS))
            link(g.memset(half_m2[0:SLOTS], -2.0))
            link(g.memset(half_m2[SLOTS:P], -1.0))
            link(g.memset(mask_row[:, 0:CHUNK], 1.0))
            link(g.memset(mask_row[:, CHUNK:P], 0.0))
            link(g.memset(mask_col[:], -1.0e30))
            link(g.memset(halves[0:64, 0:64], 1.0))
            link(g.memset(halves[0:64, 64:P], 0.0))
            link(g.memset(halves[64:P, 0:64], 0.0))
            link(g.memset(halves[64:P, 64:P], 1.0))
            for b in range(2):
                link(g.memset(u_buf[b][:, 0:PAD], 0.0))
            link(g.iota(iota_slot[:].rearrange("p (a s) -> p a s", a=2), [[0, 2], [1, SLOTS]], base=0, channel_multiplier=0, allow_small_or_imprecise_dtypes=True))
            link(g.iota(iota_tile[:], [[1, TILES]], base=0, channel_multiplier=0, allow_small_or_imprecise_dtypes=True))
            link(g.iota(iota_exp[:], [[1, EXPERTS]], base=-99, channel_multiplier=0, allow_small_or_imprecise_dtypes=True))
            link(g.iota(steps[:], [[SLOTS, STEPS]], base=SLOTS, channel_multiplier=0, allow_small_or_imprecise_dtypes=True))
            link(g.iota(assign1[:], [[1, 2], [2 * P, NT]], base=1, channel_multiplier=2, allow_small_or_imprecise_dtypes=True))
            link(g.memset(ident[:], 0.0))
            link(g.affine_select(out=ident[:], in_=ident[:], compare_op=ALU.not_equal, fill=1.0, base=0,
                                 pattern=[[-1, P]], channel_multiplier=1))
            link(g.memset(ones16[:], 1.0))
            link(g.affine_select(out=before16[:], in_=ones16[:], compare_op=ALU.is_gt, fill=0.0, base=0,
                                 pattern=[[1, P]], channel_multiplier=-1))
            g.memset(step_count[:], 0.0).then_inc(consts_ready, 1)

            k = 0
            for ct in range(NC):
                for w in range(1, POOL_TAPS):
                    k += 1
                    pool.wait_ge(tap_made, ct * POOL_TAPS + w + 1)
                    if w > 1:
                        pool.wait_ge(tap_added, k - 1)
                    g.tensor_tensor(pacc, pacc, tap[(w - 1) % 2], ALU.add).then_inc(tap_added, 1)

            def moe_rows(l):
                m, o = main[l], over[l]

                def gather(s, e, wait_at):
                    g.tensor_copy(at_in[:, s:s + 1], rows_in[:, bass.ds(e, 1)]).then_inc(at_copied[l], 1)
                    pool.wait_ge(at_copied[l], wait_at)
                    alone(pool)
                    g.indirect_dma_start(out=xe[s], out_offset=None, in_=xn_dram[l][:, :],
                                         in_offset=bass.IndirectOffsetOnAxis(ap=at_in[:, s:s + 1], axis=0),
                                         bounds_check=2 * T - 1, oob_is_err=False).then_inc(xe_loaded[l][s], 16)

                def scatter(s, e, wait_at):
                    g.tensor_copy(at_out[:, s:s + 1], rows_out[:, bass.ds(e, 1)]).then_inc(at_copied[l], 1)
                    pool.wait_ge(at_copied[l], wait_at)
                    pool.wait_ge(m["y_taken"], e + 1)
                    alone(pool)
                    g.indirect_dma_start(out=y_dram[l][:, :],
                                         out_offset=bass.IndirectOffsetOnAxis(ap=at_out[:, s:s + 1], axis=0),
                                         in_=y_sb[s], in_offset=None,
                                         bounds_check=2 * ASSIGN - 1, oob_is_err=False).then_inc(y_stored[l][s], 16)

                pool.wait_ge(lists_done, l + 1)
                pool.wait_ge(xn_stored, 16 * NT * (l + 1))
                for s in range(2):
                    link(g.memset(xe[s], 0.0))
                    gather(s, s, s + 1)
                with pool.Fori(0, EXPERTS // 2 - 1) as i:
                    for s in range(2):
                        scatter(s, i * 2 + s, i * 4 + (2 * s + 3))
                        pool.wait_ge(m["xT_ready"], i * 2 + (s + 1))
                        gather(s, i * 2 + (s + 2), i * 4 + (2 * s + 4))
                for s in range(2):
                    scatter(s, EXPERTS - 2 + s, 2 * EXPERTS - 2 + s + 1)
                n_over = pool.value_load(ctl[0:1, 0:1], min_val=0, max_val=OVER)
                with pool.If(n_over > 0):
                    with pool.Fori(0, n_over) as j:
                        pool.wait_ge(m["xT_ready"], EXPERTS)
                        pool.wait_ge(y_stored[l][0], 16 * (EXPERTS // 2))
                        g.tensor_copy(at_in[:, 0:1], rows_in[:, bass.ds(j + EXPERTS, 1)]).then_inc(at_copied_over[l], 1)
                        g.tensor_copy(at_out[:, 0:1], rows_out[:, bass.ds(j + EXPERTS, 1)]).then_inc(at_copied_over[l], 1)
                        pool.wait_ge(at_copied_over[l], j * 2 + 2)
                        alone(pool)
                        g.indirect_dma_start(out=xe[0], out_offset=None, in_=xn_dram[l][:, :],
                                             in_offset=bass.IndirectOffsetOnAxis(ap=at_in[:, 0:1], axis=0),
                                             bounds_check=2 * T - 1, oob_is_err=False).then_inc(over_xe[l], 16)
                        pool.wait_ge(o["y_taken"], j + 1)
                        alone(pool)
                        g.indirect_dma_start(out=y_dram[l][:, :],
                                             out_offset=bass.IndirectOffsetOnAxis(ap=at_out[:, 0:1], axis=0),
                                             in_=y_sb[0], in_offset=None,
                                             bounds_check=2 * ASSIGN - 1, oob_is_err=False).then_inc(over_y[l], 16)
                        pool.wait_ge(over_y[l], j * 16 + 16)
                g.memset(step_count[:, 0:1], 0.0).then_inc(moe_over, 1)

            moe_rows(0)
            moe_rows(1)

        @block.scalar
        def _(act):
            a = nc.scalar
            linked = [0]

            def link(ins):
                linked[0] += 1
                ins.then_inc(act_chain, 1)
                act.wait_ge(act_chain, linked[0])

            for l in range(LAYERS):
                act.dma_start(norm_g[:, 2 * l, :], norm1_g[l].rearrange("(h p j) -> p h j", h=2, j=4)).then_inc(params_loaded, 16)
                act.dma_start(norm_g[:, 2 * l + 1, :], norm2_g[l].rearrange("(h p j) -> p h j", h=2, j=4)).then_inc(params_loaded, 16)
            act.dma_start(chan_rows[0:TAPS, :], conv_dw[0]).then_inc(params_loaded, 16)
            for r, vec in enumerate((conv_dw_b, conv_ln_g, conv_ln_b)):
                act.dma_start(chan_rows[TAPS + r:TAPS + r + 1, :], vec).then_inc(params_loaded, 16)
            act.dma_start(chan_rows[TAPS + 3:TAPS + 5, :], conv_b_in[0].rearrange("(r n) -> r n", r=2)).then_inc(params_loaded, 16)
            act.dma_start(b_out, conv_b_out).then_inc(params_loaded, 16)
            for s, (lo, vec) in enumerate(((0, attn_q_g), (64, attn_q_g), (0, attn_k_g), (64, attn_k_g))):
                act.dma_start(qk_g[lo:lo + 64, s // 2:s // 2 + 1], vec[0].rearrange("(p o) -> p o", o=1)).then_inc(route_loaded, 16)
            act.dma_start(sub_g[:], attn_subln_g[0].rearrange("(p o) -> p o", o=1)).then_inc(route_loaded, 16)
            for s, vec in enumerate((attn_lq1, attn_lk1, attn_lq2, attn_lk2)):
                act.dma_start(lam_in[:, s, :], vec.to_broadcast([P, HEAD_DIM])).then_inc(route_loaded, 16)
            for l in range(LAYERS):
                for h in range(2):
                    rows = lambda w: w[l].rearrange("(h p j) n -> p h j n", h=2, j=4)[:, h]
                    act.dma_start(w_route[:, l, 4 * h:4 * h + 4, 0:GROUPS], rows(moe_w_grp)).then_inc(route_loaded, 16)
                    act.dma_start(w_route[:, l, 4 * h:4 * h + 4, GROUPS:ROUTES], rows(moe_w_exp)).then_inc(route_loaded, 16)
                act.dma_start(b_route[:, l, 0:GROUPS], moe_b_grp[l:l + 1, :]).then_inc(route_loaded, 16)
                act.dma_start(b_route[:, l, GROUPS:ROUTES], moe_b_exp[l:l + 1, :]).then_inc(route_loaded, 16)
            act.wait_ge(consts_ready, 1)

            def norm_stats(n):
                for t in range(NT):
                    if n == 0:
                        act.wait_ge(x_loaded, 16 * NT)
                    else:
                        act.wait_ge(x_done, 4 * (n - 1) + t + 1)
                    link(a.activation(junk, x_res[:, t, :], ACT.Square, accum_out=ssq[:, t:t + 1]))
                    a.activation(std[:, t:t + 1], ssq[:, t:t + 1], ACT.Sqrt, bias=eps[:], scale=1.0 / D).then_inc(std_done, 1)

            norm_stats(N_PRE[0])

            def squares(ct):
                act.wait_ge(conv_done, ct + 1)
                a.activation(sq_ct[:, ct, :], uT[:, ct, :], ACT.Square).then_inc(sq_done, 1)

            act.wait_ge(chan_taken, 1)
            for ct in range(NC):
                act.wait_ge(glu_ready, ct + 1)
                a.activation(sg[ct % 2], bank[2 * (ct % 2) + 1][:], ACT.Sigmoid,
                             bias=chan[:, ct, TAPS + 4:TAPS + 5]).then_inc(gate_done, 1)
                act.wait_ge(u_done, ct + 1)
                if ct >= 1:
                    act.wait_ge(conv_done, ct)
                for w in range(POOL_TAPS):
                    dst = pacc if w == 0 else tap[(w - 1) % 2]
                    if w >= 3:
                        act.wait_ge(tap_added, ct * (POOL_TAPS - 1) + w - 2)
                    a.activation(dst, u_buf[ct % 2][:, w:w + T], ACT.Copy, scale=chan[:, ct, w:w + 1]).then_inc(tap_made, 1)
                if ct >= 1:
                    squares(ct - 1)
            squares(NC - 1)
            act.wait_ge(ln_var, 1)
            a.activation(ln_r, ln_t, ACT.Sqrt, bias=eps[:]).then_inc(ln_std, 1)
            for ct in range(NC):
                act.wait_ge(ln_x, ct + 1)
                a.activation(uT[:, ct, :], uT[:, ct, :], ACT.Silu, bias=chan[:, ct, TAPS + 2:TAPS + 3],
                             scale=chan[:, ct, TAPS + 1:TAPS + 2]).then_inc(ln_done, 1)

            def route(l):
                n = N_MOE[l]
                norm_stats(n)
                for t in range(NT):
                    act.wait_ge(xn_done, 4 * n + t + 1)
                    act.dma_start(xn_dram[l][2 * t * P:2 * (t + 1) * P, :].rearrange("(p h) f -> p h f", h=2),
                                  xn[:, t, :].rearrange("p (h f) -> p h f", h=2)).then_inc(xn_stored, 16)
                act.wait_ge(exp_in, 2 * l + 1)
                a.activation(g_exp, g_dif, ACT.Exp).then_inc(exp_done, 1)
                act.wait_ge(exp_in, 2 * l + 2)
                a.activation(v4(4), v4(3), ACT.Exp).then_inc(exp_done, 1)

            def silu_of(sems, s, e1):
                act.wait_ge(sems["up_ready"], e1)
                a.activation(s_sb[s][SLOTS:P, :], bank[2 + s][0:SLOTS, :], ACT.Silu).then_inc(sems["silu_done"], 1)

            def take_y(sems, s, e1):
                act.wait_ge(sems["y_ready"], e1)
                a.activation(y_sb[s], bank[6 + s][:], ACT.Copy).then_inc(sems["y_taken"], 1)

            def experts(l):
                m = main[l]

                def pair(i, first):
                    for s in range(2):
                        silu_of(m, s, i * 2 + (s + 1))
                        if not first:
                            act.wait_ge(y_stored[l][s], i * 16)
                        take_y(m, s, i * 2 + (s + 1))

                pair(0, True)
                with act.Fori(1, EXPERTS // 2) as i:
                    pair(i, False)
                n_over = act.value_load(ctl[0:1, 0:1], min_val=0, max_val=OVER)
                with act.If(n_over > 0):
                    with act.Fori(0, n_over) as j:
                        silu_of(over[l], 0, j + 1)
                        take_y(over[l], 0, j + 1)
                for s in range(2):
                    act.wait_ge(y_stored[l][s], 16 * (EXPERTS // 2))
                act.wait_ge(moe_over, l + 1)
                for t in range(NT):
                    act.dma_start(y_in[t], y_dram[l][4 * t * P:4 * (t + 1) * P, :].rearrange("(p r) f -> p (r f)", r=4)
                                  ).then_inc(y_loaded[t], 16)

            route(0)
            act.wait_ge(lists_done, 1)
            experts(0)

            norm_stats(N_PRE[1])
            def qk_square(i):
                act.wait_ge(qk_ready, i + 1)
                if i >= 2:
                    act.wait_ge(qk_ss, i - 1)
                a.activation(qk_sqb[i % 2], bank[i % 4][:], ACT.Square).then_inc(qk_sq, 1)

            def qk_root(i):
                act.wait_ge(qk_ss, i + 1)
                if i >= 2:
                    act.wait_ge(qk_done, i - 1)
                a.activation(qk_stdb[i % 2], bank[4 + i % 2][:], ACT.Sqrt, bias=eps[:], scale=1.0 / HEAD_DIM).then_inc(qk_std, 1)

            for i in range(16):
                qk_square(i)
                if i >= 1:
                    qk_root(i - 1)
            qk_root(15)
            for i in range(2 * NT):
                act.wait_ge(v_ready, i + 1)
                a.activation(vv[:, i % NT, (i // NT) * 512:(i // NT + 1) * 512], bank[6 + i % 2][:], ACT.Copy).then_inc(v_done, 1)
            act.wait_ge(lam_sum, 1)
            a.activation(lam_t[:, 2:4], lam_t[:, 0:2], ACT.Exp).then_inc(lam_exp, 1)

            def probabilities(i):
                h, b = pairs[i]
                W = P * (b + 1)
                act.wait_ge(m_done, i + 1)
                if i >= 3:
                    act.wait_ge(a_done, i - 2)
                for c in range(2):
                    a.activation(p_sb[i % 3][:, c, 0:W], banks2[i % 3][:, c, 0:W], ACT.Exp, bias=mx[:, i, c:c + 1],
                                 accum_out=ps[:, i, c:c + 1]).then_inc(p_done, 1)

            def o_squares(i):
                h, b = pairs[i]
                act.wait_ge(o_done, i + 1)
                if i >= 1:
                    act.wait_ge(o_sq, i)
                a.activation(o_junk, o_sb[:, b, h * P:(h + 1) * P], ACT.Square,
                             accum_out=o_ssq[:, i:i + 1]).then_inc(o_sq, 1)

            def take_aT(i):
                b = pairs[i][1]
                act.wait_ge(aT_ready, i + 1)
                if i >= 2:
                    act.wait_ge(o_ready, i - 1)
                a.activation(aT[i % 2][:, 0:P * (b + 1)], bank[6][:, 0:P * (b + 1)], ACT.Copy).then_inc(aT_done, 1)

            N = len(pairs)
            probabilities(0)
            for i in range(N + 2):
                if i + 1 < N:
                    probabilities(i + 1)
                if i < N:
                    take_aT(i)
                if i >= 2:
                    o_squares(i - 2)
            act.wait_ge(o_sq, N)
            a.activation(o_std, o_ssq, ACT.Sqrt, bias=eps[:], scale=1.0 / P).then_inc(on_std, 1)

            route(1)
            act.wait_ge(lists_done, 2)
            experts(1)

        @block.vector
        def _(dve):
            v = nc.vector
            linked = [0]

            def link(ins):
                linked[0] += 1
                ins.then_inc(dve_chain, 1)
                dve.wait_ge(dve_chain, linked[0])

            def build_hT(n):
                def take(t):
                    for h in range(2):
                        m = 8 * n + 2 * t + h
                        dve.wait_ge(xt_ready, m + 1)
                        v.tensor_tensor(hT[:, 4 * h:4 * h + 4, t * P:(t + 1) * P],
                                        bank[6 + h][:].rearrange("p (j t) -> p j t", j=4),
                                        norm_g[:, n, 4 * h:4 * h + 4].unsqueeze(2).to_broadcast([P, 4, P]),
                                        ALU.mult).then_inc(xt_taken, 1)
                for t in range(NT):
                    dve.wait_ge(std_done, 4 * n + t + 1)
                    link(v.reciprocal(rstd[:, t:t + 1], std[:, t:t + 1]))
                    v.tensor_scalar(xn[:, t, :], x_res[:, t, :], rstd[:, t:t + 1], None, ALU.mult).then_inc(xn_done, 1)
                    if t >= 1:
                        take(t - 1)
                take(NT - 1)

            dve.wait_ge(consts_ready, 1)
            dve.wait_ge(params_loaded, 16 * 10)
            build_hT(N_PRE[0])
            tap_count = [0]
            dve.wait_ge(chan_ready, 1)
            link(v.tensor_copy(chan[:], bank[5][:, 0:NC * (TAPS + 5)].rearrange("p (c r) -> p c r", c=NC)))
            v.memset(small_at(20), 0.0).then_inc(chan_taken, 1)
            for ct in range(NC):
                ub = u_buf[ct % 2]
                dve.wait_ge(gate_done, ct + 1)
                if ct >= 2:
                    dve.wait_ge(tap_made, (ct - 1) * POOL_TAPS)
                v.scalar_tensor_tensor(ub[:, PAD:PAD + T], bank[2 * (ct % 2)][:], chan[:, ct, TAPS + 3:TAPS + 4], sg[ct % 2],
                                       ALU.add, ALU.mult).then_inc(u_done, 1)
                dve.wait_ge(u_done, ct + 1)
                sums = (uT[:, ct, :], acc2)
                k0 = tap_count[0]
                for k, w in enumerate(range(POOL_TAPS, TAPS)):
                    acc = sums[k % 2]
                    if k >= 2:
                        dve.wait_ge(dve_taps, k0 + k - 1)
                    if k < 2:
                        ins = v.tensor_scalar(acc, ub[:, w:w + T], chan[:, ct, w:w + 1],
                                              chan[:, ct, TAPS:TAPS + 1] if k == 0 else 0.0, ALU.mult, ALU.add)
                    else:
                        ins = v.scalar_tensor_tensor(acc, ub[:, w:w + T], chan[:, ct, w:w + 1], acc, ALU.mult, ALU.add)
                    ins.then_inc(dve_taps, 1)
                tap_count[0] += TAPS - POOL_TAPS
                dve.wait_ge(dve_taps, tap_count[0])
                link(v.tensor_tensor(uT[:, ct, :], uT[:, ct, :], acc2, ALU.add))
                dve.wait_ge(tap_added, (ct + 1) * (POOL_TAPS - 1))
                v.tensor_tensor(uT[:, ct, :], uT[:, ct, :], pacc, ALU.add).then_inc(conv_done, 1)
            dve.wait_ge(stats_ready, 1)
            link(v.tensor_scalar(ln_mu, bank[4][:], 1.0 / D, None, ALU.mult))
            link(v.tensor_tensor(ln_t, ln_mu, ln_mu, ALU.mult))
            link(v.scalar_tensor_tensor(ln_t, bank[5][:], 1.0 / D, ln_t, ALU.mult, ALU.subtract))
            v.tensor_scalar(ln_t, ln_t, 0.0, None, ALU.max).then_inc(ln_var, 1)
            dve.wait_ge(ln_std, 1)
            link(v.reciprocal(ln_r, ln_r))
            for ct in range(NC):
                link(v.tensor_tensor(uT[:, ct, :], uT[:, ct, :], ln_mu, ALU.subtract))
                v.tensor_tensor(uT[:, ct, :], uT[:, ct, :], ln_r, ALU.mult).then_inc(ln_x, 1)

            def add_mix(l):
                for t in range(NT):
                    for n in range(2):
                        k = 8 * l + 2 * t + n
                        dve.wait_ge(mix_ready, k + 1)
                        xs = x_res[:, t, n * 512:(n + 1) * 512]
                        ins = v.tensor_tensor(xs, xs, bank[n][:], ALU.add)
                        if n == 0:
                            link(ins)
                        else:
                            ins.then_inc(x_done, 1)

            def route(l):
                n = N_MOE[l]
                build_hT(n)
                bt = lambda ap, k: ap.unsqueeze(2).to_broadcast([P, ap.shape[1], k])
                dve.wait_ge(logits_ready, l + 1)
                link(v.tensor_copy(lg, bank[5][:, 0:NT * ROUTES].rearrange("p (t r) -> p t r", t=NT)))
                grp = lg[:, :, 0:GROUPS]
                iota_g = iota_exp[:, 0:GROUPS].unsqueeze(1).to_broadcast([P, NT, GROUPS])
                iota_e = iota_exp[:].unsqueeze(1).to_broadcast([P, NT, EXPERTS])
                link(v.tensor_reduce(v4(0), grp, AX.X, ALU.max))
                link(v.tensor_tensor(g_dif, grp, bt(v4(0), GROUPS), ALU.subtract))
                v.tensor_scalar(g_eq, g_dif, 0.0, None, ALU.is_ge).then_inc(exp_in, 1)
                dve.wait_ge(exp_in, 2 * l + 1)
                link(v.tensor_scalar(g_cand, g_eq, -99.0, 99.0, ALU.mult, ALU.add))
                link(v.tensor_tensor(g_cand, g_cand, iota_g, ALU.add))
                link(v.tensor_reduce(v4(1), g_cand, AX.X, ALU.min))
                link(v.tensor_tensor(g_eq, iota_g, bt(v4(1), GROUPS), ALU.is_equal))
                link(v.tensor_scalar(g_eq, g_eq, BIG, -BIG, ALU.mult, ALU.add))
                for t in range(NT):
                    link(v.tensor_tensor(sel[:, t, :].rearrange("p (g e) -> p g e", g=GROUPS),
                                         lg[:, t, GROUPS:ROUTES].rearrange("p (g e) -> p g e", g=GROUPS),
                                         bt(g_eq[:, t, :], PER_GROUP), ALU.add))
                for k in range(2):
                    top = v4(2) if k == 0 else v4(5)
                    link(v.tensor_reduce(top, sel, AX.X, ALU.max))
                    link(v.tensor_tensor(tmp, sel, bt(top, EXPERTS), ALU.is_ge))
                    link(v.tensor_scalar(tmp, tmp, -99.0, 99.0, ALU.mult, ALU.add))
                    link(v.tensor_tensor(tmp, tmp, iota_e, ALU.add))
                    link(v.tensor_reduce(v8(0)[:, k * NT:(k + 1) * NT], tmp, AX.X, ALU.min))
                    link(v.tensor_tensor(pick[k], iota_e, bt(v8(0)[:, k * NT:(k + 1) * NT], EXPERTS), ALU.is_equal))
                    if k == 0:
                        link(v.tensor_scalar(tmp, pick[0], -BIG, None, ALU.mult))
                        link(v.tensor_tensor(sel, sel, tmp, ALU.add))
                v.tensor_tensor(both, pick[0], pick[1], ALU.add).then_inc(picks_done, 1)
                v.tensor_tensor(v4(3), v4(5), v4(2), ALU.subtract).then_inc(exp_in, 1)
                dve.wait_ge(exp_done, 2 * l + 1)
                link(v.tensor_reduce(v4(6), g_exp, AX.X, ALU.add))
                dve.wait_ge(exp_done, 2 * l + 2)
                link(v.tensor_scalar(v4(7), v4(4), 1.0, None, ALU.add))
                link(v.tensor_tensor(v4(6), v4(6), v4(7), ALU.mult))
                link(v.reciprocal(gates[:, 0, :], v4(6)))
                link(v.tensor_tensor(gates[:, 1, :], gates[:, 0, :], v4(4), ALU.mult))
                dve.wait_ge(ranks_ready, l + 1)
                link(v.tensor_copy(rank, bank[4][:, 0:P].rearrange("p (t e) -> p t e", t=NT)))
                link(v.tensor_copy(count, bank[4][:, P:P + EXPERTS]))
                cmp_e = cmp.rearrange("p (e s) -> p e s", s=STEPS)
                link(v.tensor_tensor(cmp_e, bt(count, STEPS), steps[:].unsqueeze(1).to_broadcast([P, EXPERTS, STEPS]), ALU.is_gt))
                link(v.tensor_reduce(tiles_e, cmp_e, AX.X, ALU.add))
                link(v.tensor_tensor_scan(tiles_inc, ones[:, 0:EXPERTS], tiles_e, 0.0, ALU.mult, ALU.add))
                link(v.tensor_tensor(tiles_base, tiles_inc, tiles_e, ALU.subtract))
                oc = over_cmp[0:1, :].rearrange("p (j e) -> p j e", e=EXPERTS)
                link(v.tensor_tensor(oc, tiles_inc[0:1, :].unsqueeze(1).to_broadcast([1, OVER, EXPERTS]),
                                     iota_tile[0:1, 0:OVER].unsqueeze(2).to_broadcast([1, OVER, EXPERTS]), ALU.is_le))
                link(v.tensor_reduce(over_e[0:1, 1:OVER + 1], oc, AX.X, ALU.add))
                link(v.tensor_copy(over_e[0:1, 0:1], tiles_inc[0:1, EXPERTS - 1:EXPERTS]))
                link(v.tensor_scalar(ctl[:], over_e[0:1, :], float(EXPERTS), None, ALU.min))
                for k in range(2):
                    link(v.tensor_tensor(tmp, rank, pick[k], ALU.mult))
                    link(v.tensor_reduce(v8(1)[:, k * NT:(k + 1) * NT], tmp, AX.X, ALU.add))
                    link(v.tensor_tensor(tmp, pick[k], tiles_base.unsqueeze(1).to_broadcast([P, NT, EXPERTS]), ALU.mult))
                    link(v.tensor_reduce(v8(2)[:, k * NT:(k + 1) * NT], tmp, AX.X, ALU.add))
                cmp_a = cmp[:, 0:2 * NT * STEPS].rearrange("p (a s) -> p a s", s=STEPS)
                link(v.tensor_tensor(cmp_a, bt(v8(1), STEPS), steps[:].unsqueeze(1).to_broadcast([P, 2 * NT, STEPS]), ALU.is_ge))
                link(v.tensor_reduce(v8(3), cmp_a, AX.X, ALU.add))
                link(v.scalar_tensor_tensor(v8(4), v8(3), -float(SLOTS), v8(1), ALU.mult, ALU.add))
                link(v.tensor_scalar(v8(0), v8(0), 99.0, None, ALU.add))
                link(v.scalar_tensor_tensor(v8(5), v8(3), float(EXPERTS - 1), v8(2), ALU.add, ALU.add))
                link(v.tensor_tensor(v8(5), v8(5), v8(0), ALU.subtract))
                link(v.scalar_tensor_tensor(v8(5), v8(3), 0.0, v8(5), ALU.is_gt, ALU.mult))
                link(v.tensor_tensor(v8(5), v8(5), v8(0), ALU.add))
                link(v.tensor_tensor(hot_slot, iota_slot[:].unsqueeze(1).to_broadcast([P, 2 * NT, P]), bt(v8(4), P), ALU.is_equal))
                link(v.tensor_tensor(hot_tile, iota_tile[:].unsqueeze(1).to_broadcast([P, 2 * NT, TILES]), bt(v8(5), TILES), ALU.is_equal))
                v.tensor_tensor(hot_tile, hot_tile, bt(assign1[:].rearrange("p k t -> p (k t)"), TILES), ALU.mult).then_inc(hot_done, 1)
                dve.wait_ge(lists_ready, l + 1)
                link(v.tensor_scalar(list_pad, bank[4][:, 256:256 + TILES], 0.0, FAR, ALU.is_equal, ALU.mult))
                link(v.tensor_scalar(list_f, bank[4][:, 256:256 + TILES], 2.0, half_m2[:], ALU.mult, ALU.add))
                link(v.tensor_tensor(rows_out[:], list_f, list_pad, ALU.add))
                link(v.tensor_scalar(list_i, rows_out[:], 1, 0x7FFFFFFE, ALU.logical_shift_right, ALU.bitwise_and))
                link(v.tensor_scalar(list_j, rows_out[:], 1, None, ALU.bitwise_and))
                v.tensor_tensor(rows_in[:], list_i, list_j, ALU.bitwise_or).then_inc(lists_done, 1)

            def take_xT(l, sems, s, e1):
                n = N_MOE[l]
                dve.wait_ge(sems["xT_ready"], e1)
                v.tensor_tensor(xeT[s].rearrange("p j h k -> p (j h) k"),
                                bank[s][:].rearrange("p (c k) -> p c k", k=SLOTS),
                                gain_jh[n], ALU.mult).then_inc(sems["xT_taken"], 1)

            def hidden(sems, s, e1):
                dve.wait_ge(sems["silu_done"], e1)
                v.tensor_tensor(h_sb[s], s_sb[s][SLOTS:P, :], bank[2 + s][SLOTS:P, :], ALU.mult).then_inc(sems["h_done"], 1)
                dve.wait_ge(sems["hid_ready"], e1)
                v.tensor_copy(hidT[s].rearrange("p j k -> p (j k)"), bank[4 + s][:, 0:256]).then_inc(sems["hid_taken"], 1)

            gain_jh = {}
            for l in range(LAYERS):
                n = N_MOE[l]
                g8 = gain_sb[:, l, :]
                gain_jh[n] = g8.unsqueeze(2).to_broadcast([P, NC, SLOTS])

            def experts(l):
                m = main[l]

                def pair(i, first, last):
                    for s in range(2):
                        if not (last and s == 1):
                            take_xT(l, m, 1 - s, i * 2 + (s + 2))
                        hidden(m, s, i * 2 + (s + 1))

                take_xT(l, m, 0, 1)
                with dve.Fori(0, EXPERTS // 2 - 1) as i:
                    pair(i, False, False)
                pair(EXPERTS // 2 - 1, False, True)
                n_over = dve.value_load(ctl[0:1, 0:1], min_val=0, max_val=OVER)
                with dve.If(n_over > 0):
                    with dve.Fori(0, n_over) as j:
                        take_xT(l, over[l], 0, j + 1)
                        hidden(over[l], 0, j + 1)
                for t in range(NT):
                    dve.wait_ge(y_loaded[t], 16 * (l + 1))
                    for k in range(2):
                        ins = v.scalar_tensor_tensor(x_res[:, t, :], y_in[t][:, k * D:(k + 1) * D], gates[:, k, t:t + 1],
                                                     x_res[:, t, :], ALU.mult, ALU.add)
                        if k == 0:
                            link(ins)
                        else:
                            ins.then_inc(x_done, 1)

            for l in range(LAYERS):
                link(v.tensor_copy(gain_sb[:, l, :].rearrange("p (j h) -> p j h", h=2),
                                   norm_g[:, 2 * l + 1, :].rearrange("p (h j) -> p j h", h=2)))
            add_mix(0)
            route(0)
            experts(0)

            dve.wait_ge(route_loaded, ROUTE_LOADS)
            link(v.tensor_scalar(qk_g[:, 0:1], qk_g[:, 0:1], HEAD_DIM ** -0.5, None, ALU.mult))
            link(v.tensor_scalar(sub_g[:], sub_g[:], 1.0 - LAMBDA_INIT, None, ALU.mult))
            for c in range(2):
                link(v.tensor_tensor(lam_in[:, 2 * c, :], lam_in[:, 2 * c, :], lam_in[:, 2 * c + 1, :], ALU.mult))
                ins = v.tensor_reduce(lam_t[:, c:c + 1], lam_in[:, 2 * c, :], AX.X, ALU.add)
                if c == 0:
                    link(ins)
                else:
                    ins.then_inc(lam_sum, 1)
            build_hT(N_PRE[1])
            for i in range(16):
                h, is_k = 4 * (i // 8) + i % 4, (i // 4) % 2
                dst = (kT if is_k else qT)[:, h, :]
                dve.wait_ge(qk_std, i + 1)
                link(v.reciprocal(qk_rsb[i % 2], qk_stdb[i % 2]))
                v.scalar_tensor_tensor(dst, bank[i % 4][:], qk_g[:, is_k:is_k + 1], qk_rsb[i % 2],
                                       ALU.mult, ALU.mult).then_inc(qk_done, 1)
            dve.wait_ge(lam_exp, 1)
            link(v.tensor_tensor(neg_lam, lam_t[:, 3:4], lam_t[:, 2:3], ALU.subtract))
            link(v.tensor_scalar(neg_lam, neg_lam, -LAMBDA_INIT, None, ALU.add))

            def maxima(i):
                W = P * (pairs[i][1] + 1)
                dve.wait_ge(s_ready, i + 1)
                v.tensor_reduce(mx[:, i, :], banks2[i % 3][:, :, 0:W], AX.X, ALU.max, negate=True).then_inc(m_done, 1)

            def combine(i):
                W = P * (pairs[i][1] + 1)
                dve.wait_ge(p_done, 2 * i + 2)
                v.reciprocal(o_r[:, i:i + 1], ps[:, i, 0:1])
                link(v.reciprocal(r1c[:, i:i + 1], ps[:, i, 1:2]))
                link(v.tensor_scalar(r1c[:, i:i + 1], ps[:, i, 0:1], r1c[:, i:i + 1], neg_lam, ALU.mult, ALU.mult))
                if i >= 2:
                    dve.wait_ge(aT_ready, i - 1)
                v.scalar_tensor_tensor(a_sb[i % 2][:, 0:W], p_sb[i % 3][:, 1, 0:W], r1c[:, i:i + 1],
                                       p_sb[i % 3][:, 0, 0:W], ALU.mult, ALU.add).then_inc(a_done, 1)

            def take_o(i):
                h, b = pairs[i]
                dve.wait_ge(o_ready, i + 1)
                v.tensor_scalar(o_sb[:, b, h * P:(h + 1) * P], bank[7][:, 0:P], o_r[:, i:i + 1], None,
                                ALU.mult).then_inc(o_done, 1)

            N = len(pairs)
            maxima(0)
            maxima(1)
            for i in range(N + 1):
                if i < N:
                    combine(i)
                if i + 2 < N:
                    maxima(i + 2)
                if i >= 1:
                    take_o(i - 1)
            dve.wait_ge(on_std, 1)
            link(v.reciprocal(o_r, o_std))
            o_rb = o_r.rearrange("p (h b) -> p b h", b=NT)
            for b in range(NT):
                ob = o_sb[:, b, :].rearrange("p (h f) -> p h f", h=HEADS)
                v.tensor_tensor(ob, ob, o_rb[:, b, :].unsqueeze(2).to_broadcast([P, HEADS, P]), ALU.mult).then_inc(on_done, 1)
            for b in range(NT):
                for n in range(2):
                    k = 2 * b + n
                    dve.wait_ge(oT_ready, k + 1)
                    v.tensor_scalar(oT[:, 4 * n:4 * n + 4, b * P:(b + 1) * P], bank[4 + n][:].rearrange("p (h t) -> p h t", h=4),
                                    sub_g[:], None, ALU.mult).then_inc(oT_done, 1)
            add_mix(1)
            route(1)
            experts(1)

        @block.tensor
        def _(pe):
            mm = nc.tensor.matmul

            def build_hT(n):
                for t in range(NT):
                    pe.wait_ge(xn_done, 4 * n + t + 1)
                    for h in range(2):
                        m = 8 * n + 2 * t + h
                        if m >= 2:
                            pe.wait_ge(xt_taken, m - 1)
                        for j in range(4):
                            last = nc.tensor.transpose(bank[6 + h][:, j * P:(j + 1) * P],
                                                       xn[:, t, h * 512 + j:h * 512 + j + 509:4], ident[:])
                        last.then_inc(xt_ready, 1)

            def project(dst, w, src, cols, start=True, stop=True):
                for c in range(NC):
                    last = mm(dst, w[:, c, cols], src[:, c, :], start=start and c == 0, stop=stop and c == NC - 1)
                return last

            pe.wait_ge(consts_ready, 1)
            build_hT(N_PRE[0])
            pe.wait_ge(params_loaded, 16 * 10)
            R = TAPS + 5
            for ct in range(NC):
                last = nc.tensor.transpose(bank[5][:, ct * R:(ct + 1) * R], chan_rows[:, ct * P:(ct + 1) * P], ident[0:R, 0:R])
            last.then_inc(chan_ready, 1)

            def stats(ct):
                pe.wait_ge(sq_done, ct + 1)
                mm(bank[4][:], ones[:], uT[:, ct, :], start=ct == 0, stop=ct == NC - 1)
                return mm(bank[5][:], ones[:], sq_ct[:, ct, :], start=ct == 0, stop=ct == NC - 1)

            pe.wait_ge(xt_taken, 8)
            for ct in range(NC):
                ua, ug = (0, 1) if ct < 4 else (2, 3)
                loaded(pe, ua)
                loaded(pe, ug)
                if ct >= 2:
                    pe.wait_ge(u_done, ct - 1)
                cols = slice((ct % 4) * P, (ct % 4 + 1) * P)
                project(bank[2 * (ct % 2)][:], w_chunks(ua), hT, cols)
                last = project(bank[2 * (ct % 2) + 1][:], w_chunks(ug), hT, cols)
                last.then_inc(glu_ready, 1)
                if ct >= 2:
                    if ct == 2:
                        pe.wait_ge(chan_taken, 1)
                    stats(ct - 2)
            stats(NC - 2)
            stats(NC - 1).then_inc(stats_ready, 1)

            def mix_out(l, n0, src, bias):
                for n in range(2):
                    loaded(pe, n0 + n)
                for t in range(NT):
                    for n in range(2):
                        k = 8 * l + 2 * t + n
                        if t >= 1:
                            pe.wait_ge(x_done, 8 * l + t)
                        for c in range(NC):
                            if l == 0 and t == 0 and n == 0:
                                pe.wait_ge(ln_done, c + 1)
                            last = mm(bank[n][:], src[:, c, t * P:(t + 1) * P], w_chunks(n0 + n)[:, c, :],
                                      start=c == 0, stop=c == NC - 1 and not bias)
                        if bias:
                            last = mm(bank[n][:], ones[0:1, :], b_out[:, n * 512:(n + 1) * 512], start=False, stop=True)
                        last.then_inc(mix_ready, 1)

            mix_out(0, 4, uT, True)

            def route(l):
                n = N_MOE[l]
                build_hT(n)
                if l == 0:
                    pe.wait_ge(route_loaded, ROUTE_LOADS)
                for t in range(NT):
                    dst = bank[5][:, t * ROUTES:(t + 1) * ROUTES]
                    pe.wait_ge(xt_taken, 8 * n + 2 * t + 2)
                    for c in range(NC):
                        mm(dst, hT[:, c, t * P:(t + 1) * P], w_route[:, l, c, :], start=c == 0, stop=False)
                    last = mm(dst, ones[0:1, :], b_route[:, l, :], start=False, stop=True)
                last.then_inc(logits_ready, 1)
                pe.wait_ge(picks_done, l + 1)
                for t in range(NT):
                    for u in range(t + 1):
                        mm(bank[4][:, t * EXPERTS:(t + 1) * EXPERTS], ones16[:] if u < t else before16[:], both[:, u, :],
                           start=u == 0, stop=u == t)
                for u in range(NT):
                    last = mm(bank[4][:, P:P + EXPERTS], ones16[:], both[:, u, :], start=u == 0, stop=u == NT - 1)
                last.then_inc(ranks_ready, 1)
                pe.wait_ge(hot_done, l + 1)
                for a in range(2 * NT):
                    last = mm(bank[4][:, 256:256 + TILES], hot_slot[:, a, :], hot_tile[:, a, :], start=a == 0, stop=a == 2 * NT - 1)
                last.then_inc(lists_ready, 1)

            def rows_T(sems, s):
                for j in range(4):
                    last = nc.tensor.transpose(bank[s][:, j * P:(j + 1) * P], xe[s][:, j:j + 509:4], ident[:])
                last.then_inc(sems["xT_ready"], 1)

            def up(sems, s, w1u, w3u, e1):
                pe.wait_ge(sems["xT_taken"], e1)
                w1c, w3c = w_chunks(w1u), w_chunks(w3u)
                for h in range(2):
                    for j in range(4):
                        c = 4 * h + j
                        for q, w in ((0, w1c), (1, w3c)):
                            last = mm(bank[2 + s][q * SLOTS:(q + 1) * SLOTS, :], xeT[s][:, j, h, :], w[:, c, :],
                                      start=c == 0, stop=c == NC - 1)
                return last

            def hid_T(sems, s, e1):
                pe.wait_ge(sems["h_done"], e1)
                alone(pe)
                for j in range(4):
                    last = nc.tensor.transpose(bank[4 + s][:, j * SLOTS:(j + 1) * SLOTS], h_sb[s][:, j:j + 509:4],
                                               ident[0:SLOTS, 0:SLOTS])
                last.then_inc(sems["hid_ready"], 1)

            def down(sems, s, w2u, e1):
                pe.wait_ge(sems["hid_taken"], e1)
                w2c = unit(w2u).rearrange("p (j n) -> p j n", j=4)
                for j in range(4):
                    for q in range(2):
                        last = mm(bank[6 + s][q * SLOTS:(q + 1) * SLOTS, :], hidT[s][:, j, :], w2c[:, j, q * 512:(q + 1) * 512],
                                  start=j == 0, stop=j == 3)
                return last

            def experts(l):
                m = main[l]
                n0 = FIRST[l] + MIX_UNITS[l]

                def pair(i, first, last_pair):
                    for s in range(2):
                        w1u, w3u, w2u = n0 + 3 * s, n0 + 3 * s + 1, n0 + 3 * s + 2
                        pe.wait_ge(unit_loaded[w1u % RING], i * 32 + 32 * (w1u // RING + 1))
                        pe.wait_ge(unit_loaded[w3u % RING], i * 32 + 32 * (w3u // RING + 1))
                        up(m, s, w1u, w3u, i * 2 + (s + 1)).then_inc(m["up_ready"], 1)
                        if not (last_pair and s == 1):
                            nxt = 16 * s
                            pe.wait_ge(xe_loaded[l][1 - s], i * 16 + (16 + nxt))
                            rows_T(m, 1 - s)
                        hid_T(m, s, i * 2 + (s + 1))
                        pe.wait_ge(unit_loaded[w2u % RING], i * 32 + 32 * (w2u // RING + 1))
                        if not first:
                            pe.wait_ge(m["y_taken"], i * 2 + (s - 1))
                        down(m, s, w2u, i * 2 + (s + 1)).then_inc(m["y_ready"], 1)

                pe.wait_ge(xe_loaded[l][0], 16)
                rows_T(m, 0)
                pair(0, True, False)
                with pe.Fori(1, EXPERTS // 2 - 1) as i:
                    pair(i, False, False)
                pair(EXPERTS // 2 - 1, False, True)
                n_over = pe.value_load(ctl[0:1, 0:1], min_val=0, max_val=OVER)
                n1 = n0 + MOE_UNITS
                with pe.If(n_over > 0):
                    with pe.Fori(0, n_over) as j:
                        o = over[l]
                        pe.wait_ge(over_xe[l], j * 16 + 16)
                        rows_T(o, 0)
                        pe.wait_ge(over_w[l], j * 64 + 64)
                        up(o, 0, n1, n1 + 1, j + 1).then_inc(o["up_ready"], 1)
                        hid_T(o, 0, j + 1)
                        pe.wait_ge(over_w2[l], j * 32 + 32)
                        down(o, 0, n1 + 2, j + 1).then_inc(o["y_ready"], 1)

            route(0)
            pe.wait_ge(lists_done, 1)
            experts(0)

            build_hT(N_PRE[1])
            n0 = FIRST[1]
            pe.wait_ge(xt_taken, 8 * (N_PRE[1] + 1))

            def sum_squares(i):
                pe.wait_ge(qk_sq, i + 1)
                if i >= 2:
                    pe.wait_ge(qk_std, i - 1)
                mm(bank[4 + i % 2][:], halves[:], qk_sqb[i % 2], start=True, stop=True).then_inc(qk_ss, 1)

            for i in range(16):
                u = n0 + 2 * (i // 8) + (i // 4) % 2
                loaded(pe, u)
                if i >= 4:
                    pe.wait_ge(qk_done, i - 3)
                last = project(bank[i % 4][:], w_chunks(u), hT, slice((i % 4) * P, (i % 4 + 1) * P))
                last.then_inc(qk_ready, 1)
                if i >= 1:
                    sum_squares(i - 1)
            for i in range(2 * NT):
                n, t = i // NT, i % NT
                u = n0 + 4 + n
                loaded(pe, u)
                if i >= 2:
                    pe.wait_ge(v_done, i - 1)
                for c in range(NC):
                    last = mm(bank[6 + i % 2][:], hT[:, c, t * P:(t + 1) * P], w_chunks(u)[:, c, :], start=c == 0, stop=c == NC - 1)
                last.then_inc(v_ready, 1)
                if i == 0:
                    sum_squares(15)
            pe.wait_ge(qk_done, 16)
            pe.wait_ge(v_done, 2 * NT)

            def scores(i):
                h, b = pairs[i]
                W = P * (b + 1)
                if i >= 3:
                    pe.wait_ge(p_done, 2 * (i - 2))
                for c in range(2):
                    lo, hi = c * HEAD_DIM, (c + 1) * HEAD_DIM
                    mm(banks2[i % 3][:, c, 0:W], qT[lo:hi, h, b * P:(b + 1) * P], kT[lo:hi, h, 0:W], start=True, stop=False,
                       skip_group_check=True)
                for c in range(2):
                    last = mm(banks2[i % 3][:, c, W - CHUNK:W], mask_row[:], mask_col[:], start=False, stop=True,
                              skip_group_check=True)
                last.then_inc(s_ready, 1)

            def transposed(i):
                b = pairs[i][1]
                pe.wait_ge(a_done, i + 1)
                if i >= 1:
                    pe.wait_ge(aT_done, i)
                for k in range(b + 1):
                    last = nc.tensor.transpose(bank[6][:, k * P:(k + 1) * P], a_sb[i % 2][:, k * P:(k + 1) * P], ident[:])
                last.then_inc(aT_ready, 1)

            def weighted(i):
                h, b = pairs[i]
                pe.wait_ge(aT_done, i + 1)
                if i >= 1:
                    pe.wait_ge(o_done, i)
                for k in range(b + 1):
                    last = mm(bank[7][:, 0:P], aT[i % 2][:, k * P:(k + 1) * P], vv[:, k, h * P:(h + 1) * P],
                              start=k == 0, stop=k == b)
                last.then_inc(o_ready, 1)

            N = len(pairs)
            scores(0)
            scores(1)
            for i in range(N):
                if i + 2 < N:
                    scores(i + 2)
                transposed(i)
                if i >= 1:
                    weighted(i - 1)
            weighted(N - 1)
            for b in range(NT):
                pe.wait_ge(on_done, b + 1)
                for n in range(2):
                    k = 2 * b + n
                    if k >= 2:
                        pe.wait_ge(oT_done, k - 1)
                    for j in range(4):
                        h = 4 * n + j
                        last = nc.tensor.transpose(bank[4 + n][:, j * P:(j + 1) * P], o_sb[:, b, h * P:(h + 1) * P], ident[:])
                    last.then_inc(oT_ready, 1)
            pe.wait_ge(oT_done, 2 * NT)
            mix_out(1, n0 + 6, oT, False)
            route(1)
            pe.wait_ge(lists_done, 2)
            experts(1)


_INS = ["x", "norm1_g", "norm2_g", "conv_w_in", "conv_b_in", "conv_dw", "conv_dw_b", "conv_ln_g", "conv_ln_b",
        "conv_w_out", "conv_b_out", "attn_w_qkv", "attn_q_g", "attn_k_g", "attn_lq1", "attn_lk1", "attn_lq2", "attn_lk2",
        "attn_subln_g", "attn_w_o", "moe_w_grp", "moe_b_grp", "moe_w_exp", "moe_b_exp", "moe_w1", "moe_w3", "moe_w2"]


def kernel(**inputs):
    import numpy as np
    import concourse.bacc as bacc
    from concourse.bass_utils import run_bass_kernel_spmd

    nc = bacc.Bacc("TRN2", target_bir_lowering=False, num_devices=1)
    arrays, args = {}, []
    for name in _INS:
        a = np.ascontiguousarray(inputs[name])
        arrays[f"in_{name}"] = a
        args.append(nc.dram_tensor(f"in_{name}", a.shape, mybir.dt.from_np(a.dtype), kind="ExternalInput").ap())
    args.append(nc.dram_tensor("out_x", (1, T, D), F32, kind="ExternalOutput").ap())
    trunk(nc, *args)
    return run_bass_kernel_spmd(nc, [arrays], core_ids=[0]).results[0]["out_x"]
```

```python
import math
from contextlib import ExitStack

import concourse.bass as bass
from concourse import mybir

F32 = mybir.dt.float32
F16 = mybir.dt.float16
BF16 = mybir.dt.bfloat16
I32 = mybir.dt.int32
ALU = mybir.AluOpType
ACT = mybir.ActivationFunctionType
AX = mybir.AxisListType

P = 128
D = 1024
T = 512
NT = T // P
NC = D // P
EPS = 1e-6
TAPS = 31
TAP_BUFS = 3
POOL_TAPS = 12
HEADS = 8
HEAD_DIM = 64
CHUNK = 64
GROUPS = 4
PER_GROUP = 8
EXPERTS = GROUPS * PER_GROUP
D_EXPERT = 512
ROUTES = GROUPS + EXPERTS
SLOTS = 64
ASSIGN = 2 * T
OVER = (ASSIGN - 1) // (SLOTS + 1)
TILES = EXPERTS + OVER
STEPS = T // SLOTS - 1
RING = 6
UNIT = 4096
BIG = 3.0e38
FAR = 1.0e6
LAYERS = 2
MIX_UNITS = (6, 8)
EXTRA = 2
MOE_UNITS = 3 * (EXPERTS - 1)
FIRST = (0, MIX_UNITS[0] + MOE_UNITS)
ROUTE_LOADS = 16 * (12 + 6 * LAYERS)
LAMBDA_INIT = 0.8 - 0.6 * math.exp(-0.3 * 1)


def trunk(nc, x, norm1_g, norm2_g, conv_w_in, conv_b_in, conv_dw, conv_dw_b, conv_ln_g, conv_ln_b,
          conv_w_out, conv_b_out, attn_w_qkv, attn_q_g, attn_k_g, attn_lq1, attn_lk1, attn_lq2,
          attn_lk2, attn_subln_g, attn_w_o, moe_w_grp, moe_b_grp, moe_w_exp, moe_b_exp, moe_w1,
          moe_w3, moe_w2, out):
    ctx = ExitStack()

    def sb(name, shape, dt=F32):
        return ctx.enter_context(nc.sbuf_tensor(name, shape, dt))

    def sem(name):
        return ctx.enter_context(nc.semaphore(name))

    with ctx:
        x_res = sb("x_res", [P, NT, D])
        hT = sb("hT", [P, NC, T])
        ring = sb("ring", [P, RING, UNIT])
        area1 = sb("area1", [P, UNIT])
        area2 = sb("area2", [P, UNIT])
        area3 = sb("area3", [P, UNIT])
        scratch = sb("scratch", [P, 5632])
        ident = sb("ident", [P, P])
        ones = sb("ones", [P, P])
        halves = sb("halves", [P, P])
        iota_slot = sb("iota_slot", [P, P])
        iota_tile = sb("iota_tile", [P, TILES])
        iota_exp = sb("iota_exp", [P, EXPERTS])
        steps = sb("steps", [P, STEPS])
        step_count = sb("step_count", [P, 2 * NT])
        assign1 = sb("assign1", [P, 2, NT])
        half_m2 = sb("half_m2", [P, 1])
        eps = sb("eps", [P, 1])
        mask_row = sb("mask_row", [1, P], BF16)
        mask_col = sb("mask_col", [1, CHUNK], BF16)
        ones16 = sb("ones16", [P, P], F16)
        before16 = sb("before16", [P, P], F16)
        norm_g = sb("norm_g", [P, 2 * LAYERS, NC])
        w_route = sb("w_route", [P, LAYERS, NC, ROUTES])
        b_route = sb("b_route", [1, LAYERS, ROUTES])
        chan = sb("chan", [P, NC, TAPS + 5])
        qk_g = sb("qk_g", [P, 2])
        sub_g = sb("sub_g", [P, 1])
        lam_in = sb("lam_in", [P, 4, HEAD_DIM])
        small = sb("small", [P, 64])
        gates = sb("gates", [P, 2, NT])
        gain_sb = sb("gain_sb", [P, LAYERS, NC])
        ctl = sb("ctl", [1, 1 + OVER], I32)
        rows_in = sb("rows_in", [P, TILES], I32)
        rows_out = sb("rows_out", [P, TILES], I32)
        at_in = sb("at_in", [P, 2], I32)
        at_out = sb("at_out", [P, 2], I32)
        banks2 = [ctx.enter_context(nc.psum_tensor(f"banks{2 * i}_{2 * i + 1}", [P, 2, 512], F32)) for i in range(4)]
        bank = [banks2[i // 2][:, i % 2, :] for i in range(8)]

        xn_dram = [nc.dram_tensor(f"xn_dram{l}", [2 * T, D // 2], F32, kind="Internal").ap() for l in range(LAYERS)]
        y_dram = [nc.dram_tensor(f"y_dram{l}", [2 * ASSIGN, D // 2], F32, kind="Internal").ap() for l in range(LAYERS)]

        def small_at(a, n=1):
            return small[:, a:a + n]

        ssq, std, rstd = small_at(0, NT), small_at(4, NT), small_at(8, NT)

        consts_ready, params_loaded, x_loaded = sem("consts_ready"), sem("params_loaded"), [sem(f"x_loaded{t}") for t in range(NT)]
        gain_loaded, route_loaded = sem("gain_loaded"), sem("route_loaded")
        unit_loaded = [sem(f"unit_loaded{i}") for i in range(RING)]
        extra_loaded = [sem(f"extra_loaded{k}") for k in range(3)]
        dve_chain, dve_taps = sem("dve_chain"), sem("dve_taps")
        act_chain = sem("act_chain")
        pool_chain = sem("pool_chain")
        ssq_done, std_done, xn_done = sem("ssq_done"), sem("std_done"), sem("xn_done")
        rstd_done = sem("rstd_done")
        xt_ready, xt_taken = sem("xt_ready"), sem("xt_taken")
        x_done = sem("x_done")
        chan_ready, chan_taken = sem("chan_ready"), sem("chan_taken")
        glu_ready, gate_done, u_done = sem("glu_ready"), sem("gate_done"), sem("u_done")
        tap_made, tap_added, conv_done, sq_done = sem("tap_made"), sem("tap_added"), sem("conv_done"), sem("sq_done")
        stats_ready, ln_var, ln_std, ln_x, ln_done = sem("stats_ready"), sem("ln_var"), sem("ln_std"), sem("ln_x"), sem("ln_done")
        mix_ready = sem("mix_ready")
        xn_stored, logits_ready, exp_in, exp_done = sem("xn_stored"), sem("logits_ready"), sem("exp_in"), sem("exp_done")
        picks_done, ranks_ready, hot_done, lists_ready, lists_done = (
            sem("picks_done"), sem("ranks_ready"), sem("hot_done"), sem("lists_ready"), sem("lists_done"))
        qk_ready, qk_sq, qk_ss, qk_root, qk_rec, qk_rs_ready, qk_scaled, qk_done = (
            sem("qk_ready"), sem("qk_sq"), sem("qk_ss"), sem("qk_root"), sem("qk_rec"), sem("qk_rs_ready"),
            sem("qk_scaled"), sem("qk_done"))
        v_ready, v_done = sem("v_ready"), sem("v_done")
        s_ready, m_done, p_done, a_done = sem("s_ready"), sem("m_done"), sem("p_done"), sem("a_done")
        aT_ready, aT_done, o_ready, o_done, o_sq = sem("aT_ready"), sem("aT_done"), sem("o_ready"), sem("o_done"), sem("o_sq")
        on_std, on_done, oT_ready, oT_done = sem("on_std"), sem("on_done"), sem("oT_ready"), sem("oT_done")
        lam_sum, lam_exp = sem("lam_sum"), sem("lam_exp")
        names = ("xT_ready", "xT_taken", "up_ready", "silu_done", "h_done", "hid_ready", "hid_taken", "y_ready", "y_taken")
        main = [{n: sem(f"{n}_main{l}") for n in names} for l in range(LAYERS)]
        over = [{n: sem(f"{n}_over{l}") for n in names} for l in range(LAYERS)]
        xe_loaded = [[sem(f"xe_loaded{l}_{s}") for s in range(2)] for l in range(LAYERS)]
        y_stored = [[sem(f"y_stored{l}_{s}") for s in range(2)] for l in range(LAYERS)]
        over_xe = [sem(f"over_xe{l}") for l in range(LAYERS)]
        over_y = [sem(f"over_y{l}") for l in range(LAYERS)]
        over_w = [sem(f"over_w{l}") for l in range(LAYERS)]
        over_w2 = [sem(f"over_w2{l}") for l in range(LAYERS)]
        at_copied = [sem(f"at_copied{l}") for l in range(LAYERS)]
        at_copied_over = [sem(f"at_copied_over{l}") for l in range(LAYERS)]
        moe_over = sem("moe_over")
        waits_alone = sem("waits_alone")
        y_loaded = [sem(f"y_loaded{t}") for t in range(NT)]
        out_stored = sem("out_stored")

        def alone(eng):
            eng.sem_inc(waits_alone, 1)

        block = ctx.enter_context(nc.Block())

        def unit(n):
            return ring[:, n % RING, :]

        def loaded(eng, n):
            eng.wait_ge(unit_loaded[n % RING], 32 * (n // RING + 1))

        def cols_dram(w, c0, width=512):
            v = w[:, c0:c0 + width].rearrange("(h p j) n -> h p j n", h=2, j=4)
            return [v[h] for h in range(2)]

        def rows_dram(w, c0, width=512):
            v = w[:, c0:c0 + width].rearrange("(h c p) n -> h p c n", h=2, p=P)
            return [v[h] for h in range(2)]

        def w_chunks(n):
            return unit(n).rearrange("p (c n) -> p c n", c=NC)

        xn = area1[:].rearrange("p (t f) -> p t f", t=NT)
        sq_ct = area1[:].rearrange("p (c t) -> p c t", c=NC)
        uT = area2[:].rearrange("p (c t) -> p c t", c=NC)
        chan_rows = area3[0:TAPS + 5, 0:D]
        b_out = area3[0:1, 3072:3072 + D]
        PAD = TAPS - 1
        u_buf = [scratch[:, b * (T + PAD):(b + 1) * (T + PAD)] for b in range(2)]
        base = 2 * (T + PAD)
        sg = [scratch[:, base + b * T:base + (b + 1) * T] for b in range(2)]
        tap = [scratch[:, base + (2 + b) * T:base + (3 + b) * T] for b in range(TAP_BUFS)]
        pacc = [scratch[:, base + (5 + b) * T:base + (6 + b) * T] for b in range(2)]
        acc2 = scratch[:, base + 7 * T:base + 8 * T]
        ln_mu = area3[:, 1024:1024 + T]
        ln_r = area3[:, 1024 + T:1024 + 2 * T]
        ln_t = area3[:, 1024 + 2 * T:1024 + 3 * T]
        xe = [scratch[:, s * 512:(s + 1) * 512] for s in range(2)]
        xeT = [scratch[:, 1024 + s * 512:1536 + s * 512].rearrange("p (j h k) -> p j h k", j=4, h=2) for s in range(2)]
        s_sb = [scratch[:, 2048 + s * 512:2560 + s * 512] for s in range(2)]
        h_sb = [scratch[0:SLOTS, 3072 + s * 512:3584 + s * 512] for s in range(2)]
        hidT = [scratch[:, 4096 + s * 256:4352 + s * 256].rearrange("p (j k) -> p j k", j=4) for s in range(2)]
        y_sb = [scratch[:, 4608 + s * 512:5120 + s * 512] for s in range(2)]
        extra_units = (area3[:], hT[:].rearrange("p c t -> p (c t)"), area1[:])
        ahead_unit = area2[:]
        r2 = lambda a, n: scratch[:, 3264 + a:3264 + a + n]
        lg_g = r2(0, NT * GROUPS).rearrange("p (t g) -> p t g", t=NT)
        lg_e = r2(16, NT * EXPERTS)
        sel = r2(256, NT * EXPERTS).rearrange("p (t e) -> p t e", t=NT)
        tmp = r2(384, NT * EXPERTS).rearrange("p (t e) -> p t e", t=NT)
        picks = r2(512, 256)
        tmp2 = scratch[:, 1024:1280]
        pick = [r2(512 + 128 * k, 128).rearrange("p (t e) -> p t e", t=NT) for k in range(2)]
        both = r2(768, 64).bitcast(F16).rearrange("p (t e) -> p t e", t=NT)
        rank = r2(896, 128).rearrange("p (t e) -> p t e", t=NT)
        count = r2(1024, EXPERTS)
        tiles_e = r2(1056, EXPERTS)
        tiles_inc = r2(1088, EXPERTS)
        tiles_base = r2(1120, EXPERTS)
        cmp = r2(1152, EXPERTS * STEPS)
        g_eq = r2(1376, NT * GROUPS).rearrange("p (t g) -> p t g", t=NT)
        g_cand = r2(1392, NT * GROUPS).rearrange("p (t g) -> p t g", t=NT)
        g_dif = r2(1408, NT * GROUPS).rearrange("p (t g) -> p t g", t=NT)
        g_exp = r2(1424, NT * GROUPS).rearrange("p (t g) -> p t g", t=NT)
        v4 = lambda k: r2(1440 + NT * k, NT)
        v8 = lambda k: r2(1504 + 2 * NT * k, 2 * NT)
        over_cmp = r2(1600, OVER * EXPERTS)
        over_e = r2(2080, OVER + 1)
        list_f = r2(2100, TILES)
        list_pad = r2(2150, TILES)
        list_i = r2(2200, TILES).bitcast(I32)
        list_j = r2(2250, TILES).bitcast(I32)
        hot_slot = scratch[:, 2048:2048 + NT * P].bitcast(F16).rearrange("p (k s) -> p k s", k=2 * NT)
        hot_tile = scratch[:, 3072:3072 + NT * TILES].bitcast(F16).rearrange("p (k s) -> p k s", k=2 * NT)
        y_in = [(area1, area2)[t // 2][:, (t % 2) * 2048:(t % 2 + 1) * 2048] for t in range(NT)]
        ring3 = [area3[:, b * T:(b + 1) * T] for b in range(8)]
        qT, kT = ring3[0:2], ring3[2:4]
        vh = [r.rearrange("p (b f) -> p b f", b=NT) for r in ring3[4:6]]
        oh = [r.rearrange("p (b f) -> p b f", b=NT) for r in ring3[6:8]]
        oT = area2[:].rearrange("p (h t) -> p h t", h=HEADS)
        qk_sqb = [area1[:, c * T:(c + 1) * T] for c in range(2)]
        qk_rs_wide = [area1[:, (4 + c) * T:(5 + c) * T] for c in range(2)]
        qk_g_sb = [area1[:, (2 + c) * T:(3 + c) * T] for c in range(2)]
        p_sb = [scratch[:, b * 1024:(b + 1) * 1024].rearrange("p (c k) -> p c k", c=2) for b in range(3)]
        a_sb = [scratch[:, 3072 + b * 512:3584 + b * 512] for b in range(2)]
        aT = [scratch[:, 4096 + b * 512:4608 + b * 512] for b in range(2)]
        junk = scratch[:, 4608:5632]
        pairs = [(h, b) for h in range(HEADS) for b in range(NT)]
        score = banks2[0]
        qk_bank = [bank[2], bank[3]]
        ss_bank = bank[4][:, 0:4 * NT]
        rs_bank = [bank[4], bank[1]]
        v_bank, aT_bank, o_bank = bank[5], bank[6], bank[7]
        mx = scratch[:, 5120:5120 + 64].rearrange("p (i c) -> p i c", c=2)
        ps = scratch[:, 5184:5184 + 64].rearrange("p (i c) -> p i c", c=2)
        r1c = scratch[:, 5248:5248 + 32]
        o_ssq = scratch[:, 5280:5280 + 32]
        o_std = scratch[:, 5312:5312 + 32]
        o_r = scratch[:, 5344:5344 + 32]
        o_rn = scratch[:, 5376:5376 + 32]
        o_junk = scratch[:, 5408:5408 + P]
        qk_std = scratch[:, 5536:5536 + 4 * NT]
        qk_rs = scratch[:, 5552:5552 + 4 * NT]

        ahead = (0, 4)

        def mix_bank(l, k):
            return bank[k % 4 + 2 * l]

        logit_bank = (bank[5], bank[1])

        def attention_steps():
            for st in range(HEADS + 2):
                yield tuple(x if 0 <= x < HEADS else None for x in (st, st - 1, st - 2))

        neg_lam = small_at(12)
        lam_t = small_at(13, 4)
        N_PRE = (0, 2)
        N_MOE = (1, 3)

        @block.sync
        def _(sp):
            def load_unit(dst, halves, done):
                for h in range(2):
                    sp.dma_start(dst[h], halves[h]).then_inc(done, 16)

            def chunk_halves(u):
                return [u[:, h * UNIT // 2:(h + 1) * UNIT // 2].rearrange("p (c n) -> p c n", c=4) for h in range(2)]

            def flat_halves(u):
                return [u[:, h * UNIT // 2:(h + 1) * UNIT // 2] for h in range(2)]

            def mix_unit(n, src):
                load_unit(chunk_halves(unit(n)), src, unit_loaded[n % RING])

            def moe_weights(l, freed, meanwhile):
                n0 = FIRST[l] + MIX_UNITS[l]
                w1v = moe_w1[l].rearrange("e (h p j) n -> e h p (j n)", h=2, j=4)
                w3v = moe_w3[l].rearrange("e (h p j) n -> e h p (j n)", h=2, j=4)
                w2v = moe_w2[l].rearrange("e (p h j) n -> e h p (j n)", h=2, j=2)

                def expert_units(e):
                    return [[w[e, h] for h in range(2)] for w in (w1v, w3v, w2v)]

                def load_expert(e, ring_place, freed, count=3):
                    for k, src in enumerate(expert_units(e)[:count]):
                        n = n0 + 3 * ring_place + k
                        sp.wait_ge(*freed[k])
                        load_unit(flat_halves(unit(n)), src, unit_loaded[n % RING])

                def used(count):
                    return [(main[l]["up_ready"], count)] * 2 + [(main[l]["y_ready"], count)]

                load_expert(0, 0, freed[0:3])
                load_expert(1, 1, freed[3:6])
                extra_free = ((mix_ready, 8 * (l + 1)), (logits_ready, l + 1), (xn_stored, 16 * NT * (l + 1)))
                for k, src in enumerate(expert_units(EXTRA)):
                    sp.wait_ge(*extra_free[k])
                    load_unit(flat_halves(extra_units[k]), src, extra_loaded[k])
                n = n0 + 3 * EXTRA + 2
                sp.wait_ge(xe_loaded[l][1], 16)
                load_unit(flat_halves(ahead_unit), expert_units(EXTRA + 1)[2], unit_loaded[n % RING])
                load_expert(3, 2, used(1), 2)
                load_expert(4, 3, used(2))
                with sp.Fori(2, EXPERTS // 2 - 1) as i:
                    for s in range(2):
                        load_expert(i * 2 + (s + 1), s, used(i * 2 + s))
                load_expert(EXPERTS - 1, EXPERTS - 2, used(EXPERTS - 2))
                sp.wait_ge(lists_done, l + 1)
                n_over = sp.value_load(ctl[0:1, 0:1], min_val=0, max_val=OVER)

                def over_tile(j, freed=None):
                    e = sp.value_load(ctl[0:1, bass.ds(j + 1, 1)], min_val=0, max_val=EXPERTS - 1)
                    for k, w in enumerate(expert_units(e)):
                        if freed:
                            sp.wait_ge(*freed[k])
                        load_unit(flat_halves(unit(n0 + MOE_UNITS + k)), w, over_w[l] if k < 2 else over_w2[l])

                with sp.If(n_over > 0):
                    over_tile(0, used(EXPERTS - 1))
                meanwhile()
                with sp.If(n_over > 1):
                    with sp.Fori(1, n_over) as j:
                        sp.wait_ge(over[l]["y_ready"], j)
                        alone(sp)
                        over_tile(j)

            w_in, w_out = conv_w_in[0], conv_w_out[0]
            for t in range(NT):
                sp.dma_start(x_res[:, t, :], x[0, t * P:(t + 1) * P, :]).then_inc(x_loaded[t], 16)
                if t == 0:
                    sp.dma_start(norm_g[:, 0, :], norm1_g[0].rearrange("(h p j) -> p h j", h=2, j=4)).then_inc(gain_loaded, 16)
            mix_unit(0, cols_dram(w_in, 0))
            mix_unit(1, cols_dram(w_in, D))
            sp.dma_start(chan_rows[0:TAPS, :], conv_dw[0]).then_inc(params_loaded, 16)
            for r, vec in enumerate((conv_dw_b, conv_ln_g, conv_ln_b)):
                sp.dma_start(chan_rows[TAPS + r:TAPS + r + 1, :], vec).then_inc(params_loaded, 16)
            sp.dma_start(chan_rows[TAPS + 3:TAPS + 5, :], conv_b_in[0].rearrange("(r n) -> r n", r=2)).then_inc(params_loaded, 16)
            sp.dma_start(b_out, conv_b_out).then_inc(params_loaded, 16)
            mix_unit(2, cols_dram(w_in, 512))
            mix_unit(3, cols_dram(w_in, D + 512))
            for n in range(2):
                mix_unit(4 + n, rows_dram(w_out, n * 512))
            for n, g in ((1, norm2_g[0]), (2, norm1_g[1]), (3, norm2_g[1])):
                sp.dma_start(norm_g[:, n, :], g.rearrange("(h p j) -> p h j", h=2, j=4)).then_inc(route_loaded, 16)
            for s, (lo, vec) in enumerate(((0, attn_q_g), (64, attn_q_g), (0, attn_k_g), (64, attn_k_g))):
                sp.dma_start(qk_g[lo:lo + 64, s // 2:s // 2 + 1], vec[0].rearrange("(p o) -> p o", o=1)).then_inc(route_loaded, 16)
            sp.dma_start(sub_g[:], attn_subln_g[0].rearrange("(p o) -> p o", o=1)).then_inc(route_loaded, 16)
            for s, vec in enumerate((attn_lq1, attn_lk1, attn_lq2, attn_lk2)):
                sp.dma_start(lam_in[:, s, :], vec.to_broadcast([P, HEAD_DIM])).then_inc(route_loaded, 16)
            for l in range(LAYERS):
                for h in range(2):
                    rows = lambda w: w[l].rearrange("(h p j) n -> p h j n", h=2, j=4)[:, h]
                    sp.dma_start(w_route[:, l, 4 * h:4 * h + 4, 0:GROUPS], rows(moe_w_grp)).then_inc(route_loaded, 16)
                    sp.dma_start(w_route[:, l, 4 * h:4 * h + 4, GROUPS:ROUTES], rows(moe_w_exp)).then_inc(route_loaded, 16)
                sp.dma_start(b_route[:, l, 0:GROUPS], moe_b_grp[l:l + 1, :]).then_inc(route_loaded, 16)
                sp.dma_start(b_route[:, l, GROUPS:ROUTES], moe_b_exp[l:l + 1, :]).then_inc(route_loaded, 16)
            n0 = FIRST[1]
            w_qkv, w_o = attn_w_qkv[0], attn_w_o[0]
            qkv_cols = (0, D, 2 * D, 512, D + 512, 2 * D + 512)
            done = main[0]

            def qkv_unit(n):
                if n >= 3:
                    sp.wait_ge(done["up_ready" if n < 5 else "y_ready"], EXPERTS)
                mix_unit(n0 + n, cols_dram(w_qkv, qkv_cols[n]))

            moe_weights(0, [(glu_ready, 4)] * 2 + [(glu_ready, 8)] * 2 + [(mix_ready, 8)] * 2, lambda: qkv_unit(3))
            sp.wait_ge(moe_over, 1)
            for t in range(NT):
                sp.wait_ge(y_loaded[t], 16)
            for n in (0, 1, 2, 4, 5):
                qkv_unit(n)
            sp.wait_ge(qk_ready, 8)
            for n in range(2):
                mix_unit(n0 + 6 + n, rows_dram(w_o, n * 512))
            moe_weights(1, [(v_ready, 4), (qk_ready, 15), (qk_ready, 16), (v_ready, 8)] + [(mix_ready, 16)] * 2,
                        lambda: None)
            for t in range(NT):
                sp.wait_ge(x_done, 12 + t + 1)
                sp.dma_start(out[0, t * P:(t + 1) * P, :], x_res[:, t, :]).then_inc(out_stored, 16)
            sp.wait_ge(out_stored, 16 * NT)

        @block.gpsimd
        def _(pool):
            g = nc.gpsimd
            linked = [0]

            def link(ins):
                linked[0] += 1
                ins.then_inc(pool_chain, 1)
                pool.wait_ge(pool_chain, linked[0])

            link(g.memset(ones[:], 1.0))
            link(g.memset(eps[:], EPS))
            link(g.memset(half_m2[0:SLOTS], -2.0))
            link(g.memset(half_m2[SLOTS:P], -1.0))
            link(g.memset(mask_row[:, 0:CHUNK], 1.0))
            link(g.memset(mask_row[:, CHUNK:P], 0.0))
            link(g.memset(mask_col[:], -1.0e30))
            link(g.memset(halves[0:64, 0:64], 1.0))
            link(g.memset(halves[0:64, 64:P], 0.0))
            link(g.memset(halves[64:P, 0:64], 0.0))
            link(g.memset(halves[64:P, 64:P], 1.0))
            for b in range(2):
                link(g.memset(u_buf[b][:, 0:PAD], 0.0))
            link(g.iota(iota_slot[:].rearrange("p (a s) -> p a s", a=2), [[0, 2], [1, SLOTS]], base=0, channel_multiplier=0, allow_small_or_imprecise_dtypes=True))
            link(g.iota(iota_tile[:], [[1, TILES]], base=0, channel_multiplier=0, allow_small_or_imprecise_dtypes=True))
            link(g.iota(iota_exp[:], [[1, EXPERTS]], base=-99, channel_multiplier=0, allow_small_or_imprecise_dtypes=True))
            link(g.iota(steps[:], [[SLOTS, STEPS]], base=SLOTS, channel_multiplier=0, allow_small_or_imprecise_dtypes=True))
            link(g.iota(assign1[:], [[1, 2], [2 * P, NT]], base=1, channel_multiplier=2, allow_small_or_imprecise_dtypes=True))
            link(g.memset(ident[:], 0.0))
            link(g.affine_select(out=ident[:], in_=ident[:], compare_op=ALU.not_equal, fill=1.0, base=0,
                                 pattern=[[-1, P]], channel_multiplier=1))
            link(g.memset(ones16[:], 1.0))
            link(g.affine_select(out=before16[:], in_=ones16[:], compare_op=ALU.is_gt, fill=0.0, base=0,
                                 pattern=[[1, P]], channel_multiplier=-1))
            g.memset(step_count[:], 0.0).then_inc(consts_ready, 1)

            k = 0
            for ct in range(NC):
                for w in range(1, POOL_TAPS):
                    k += 1
                    pool.wait_ge(tap_made, ct * POOL_TAPS + w + 1)
                    if w > 1:
                        pool.wait_ge(tap_added, k - 1)
                    g.tensor_tensor(pacc[ct % 2], pacc[ct % 2], tap[(k - 1) % TAP_BUFS], ALU.add).then_inc(tap_added, 1)

            def moe_rows(l):
                m, o = main[l], over[l]

                def gather(s, e, wait_at):
                    g.tensor_copy(at_in[:, s:s + 1], rows_in[:, bass.ds(e, 1)]).then_inc(at_copied[l], 1)
                    pool.wait_ge(at_copied[l], wait_at)
                    alone(pool)
                    g.indirect_dma_start(out=xe[s], out_offset=None, in_=xn_dram[l][:, :],
                                         in_offset=bass.IndirectOffsetOnAxis(ap=at_in[:, s:s + 1], axis=0),
                                         bounds_check=2 * T - 1, oob_is_err=False).then_inc(xe_loaded[l][s], 16)

                def scatter(s, e, wait_at):
                    pool.wait_ge(m["y_taken"], e + 1)
                    alone(pool)
                    g.tensor_copy(at_out[:, s:s + 1], rows_out[:, bass.ds(e, 1)]).then_inc(at_copied[l], 1)
                    pool.wait_ge(at_copied[l], wait_at)
                    alone(pool)
                    g.indirect_dma_start(out=y_dram[l][:, :],
                                         out_offset=bass.IndirectOffsetOnAxis(ap=at_out[:, s:s + 1], axis=0),
                                         in_=y_sb[s], in_offset=None,
                                         bounds_check=2 * ASSIGN - 1, oob_is_err=False).then_inc(y_stored[l][s], 16)

                pool.wait_ge(x_done, 8 * l + 4)
                for s in range(2):
                    link(g.memset(xe[s], 0.0))
                pool.wait_ge(lists_done, l + 1)
                pool.wait_ge(xn_stored, 16 * NT * (l + 1))
                for s in range(2):
                    gather(s, s, s + 1)

                def next_rows(e, s, wait_at):
                    pool.wait_ge(m["xT_ready"], e - 1)
                    gather(s, e, wait_at)

                next_rows(2, 0, 3)
                with pool.Fori(0, EXPERTS // 2 - 2) as i:
                    for s in range(2):
                        next_rows(i * 2 + (s + 3), 1 - s, i * 4 + (2 * s + 4))
                        scatter(s, i * 2 + s, i * 4 + (2 * s + 5))
                next_rows(EXPERTS - 1, 1, 2 * EXPERTS - 4)
                scatter(0, EXPERTS - 4, 2 * EXPERTS - 3)

                def over_gather(j):
                    g.tensor_copy(at_in[:, 0:1], rows_in[:, bass.ds(j + EXPERTS, 1)]).then_inc(at_copied_over[l], 1)
                    pool.wait_ge(at_copied_over[l], j * 2 + 1)
                    alone(pool)
                    g.indirect_dma_start(out=xe[0], out_offset=None, in_=xn_dram[l][:, :],
                                         in_offset=bass.IndirectOffsetOnAxis(ap=at_in[:, 0:1], axis=0),
                                         bounds_check=2 * T - 1, oob_is_err=False).then_inc(over_xe[l], 16)

                def over_scatter(j):
                    g.tensor_copy(at_out[:, 0:1], rows_out[:, bass.ds(j + EXPERTS, 1)]).then_inc(at_copied_over[l], 1)
                    pool.wait_ge(at_copied_over[l], j * 2 + 2)
                    pool.wait_ge(o["y_taken"], j + 1)
                    alone(pool)
                    g.indirect_dma_start(out=y_dram[l][:, :],
                                         out_offset=bass.IndirectOffsetOnAxis(ap=at_out[:, 0:1], axis=0),
                                         in_=y_sb[0], in_offset=None,
                                         bounds_check=2 * ASSIGN - 1, oob_is_err=False).then_inc(over_y[l], 16)
                    pool.wait_ge(over_y[l], j * 16 + 16)

                n_over = pool.value_load(ctl[0:1, 0:1], min_val=0, max_val=OVER)
                with pool.If(n_over > 0):
                    pool.wait_ge(m["xT_ready"], EXPERTS - 1)
                    over_gather(0)
                for e in range(EXPERTS - 3, EXPERTS):
                    scatter(e % 2, e, EXPERTS + e + 1)
                with pool.If(n_over > 0):
                    pool.wait_ge(y_stored[l][0], 16 * (EXPERTS // 2))
                    over_scatter(0)
                with pool.If(n_over > 1):
                    with pool.Fori(1, n_over) as j:
                        over_gather(j)
                        over_scatter(j)
                g.memset(step_count[:, 0:1], 0.0).then_inc(moe_over, 1)

            moe_rows(0)
            moe_rows(1)

        @block.scalar
        def _(act):
            a = nc.scalar
            linked = [0]

            def link(ins):
                linked[0] += 1
                ins.then_inc(act_chain, 1)
                act.wait_ge(act_chain, linked[0])

            act.wait_ge(consts_ready, 1)

            def norm_stats(n, t):
                if n == 0:
                    act.wait_ge(x_loaded[t], 16)
                else:
                    act.wait_ge(x_done, 4 * (n - 1) + t + 1)
                link(a.activation(junk, x_res[:, t, :], ACT.Square, accum_out=ssq[:, t:t + 1]))
                a.activation(std[:, t:t + 1], ssq[:, t:t + 1], ACT.Sqrt, bias=eps[:], scale=1.0 / D).then_inc(std_done, 1)

            def normalise(n, t):
                act.wait_ge(rstd_done, 4 * n + t + 1)
                a.activation(xn[:, t, :], x_res[:, t, :], ACT.Copy, scale=rstd[:, t:t + 1]).then_inc(xn_done, 1)

            for t in range(NT):
                norm_stats(N_PRE[0], t)
                normalise(N_PRE[0], t)

            def squares(ct):
                act.wait_ge(conv_done, ct + 1)
                a.activation(sq_ct[:, ct, :], uT[:, ct, :], ACT.Square).then_inc(sq_done, 1)

            act.wait_ge(chan_taken, 1)

            def gate(ct):
                act.wait_ge(glu_ready, ct + 1)
                a.activation(sg[ct % 2], bank[2 * (ct % 2) + 1][:], ACT.Sigmoid,
                             bias=chan[:, ct, TAPS + 4:TAPS + 5]).then_inc(gate_done, 1)

            gate(0)
            for ct in range(NC):
                act.wait_ge(u_done, ct + 1)
                if ct >= 2:
                    act.wait_ge(conv_done, ct - 1)
                for w in range(POOL_TAPS):
                    k = ct * (POOL_TAPS - 1) + w - 1
                    dst = pacc[ct % 2] if w == 0 else tap[k % TAP_BUFS]
                    if w >= 1 and k >= TAP_BUFS:
                        act.wait_ge(tap_added, k - TAP_BUFS + 1)
                    a.activation(dst, u_buf[ct % 2][:, w:w + T], ACT.Copy, scale=chan[:, ct, w:w + 1]).then_inc(tap_made, 1)
                    if w == POOL_TAPS // 2 and ct + 1 < NC:
                        gate(ct + 1)
                if ct >= 1:
                    squares(ct - 1)
            squares(NC - 1)
            act.wait_ge(ln_var, 1)
            a.activation(ln_r, ln_t, ACT.Sqrt, bias=eps[:]).then_inc(ln_std, 1)
            for ct in range(NC):
                act.wait_ge(ln_x, ct + 1)
                a.activation(uT[:, ct, :], uT[:, ct, :], ACT.Silu, bias=chan[:, ct, TAPS + 2:TAPS + 3],
                             scale=chan[:, ct, TAPS + 1:TAPS + 2]).then_inc(ln_done, 1)

            def route(l):
                n = N_MOE[l]
                for t in range(NT):
                    norm_stats(n, t)
                    normalise(n, t)
                    act.wait_ge(xn_done, 4 * n + t + 1)
                    act.dma_start(xn_dram[l][2 * t * P:2 * (t + 1) * P, :].rearrange("(p h) f -> p h f", h=2),
                                  xn[:, t, :].rearrange("p (h f) -> p h f", h=2)).then_inc(xn_stored, 16)
                act.wait_ge(exp_in, 2 * l + 1)
                a.activation(g_exp, g_dif, ACT.Exp).then_inc(exp_done, 1)
                act.wait_ge(exp_in, 2 * l + 2)
                a.activation(v4(4), v4(3), ACT.Exp).then_inc(exp_done, 1)

            def silu_of(sems, s, e1):
                act.wait_ge(sems["up_ready"], e1)
                a.activation(s_sb[s][SLOTS:P, :], bank[2 + s][0:SLOTS, :], ACT.Silu).then_inc(sems["silu_done"], 1)

            def take_y(sems, s, e1):
                act.wait_ge(sems["y_ready"], e1)
                a.activation(y_sb[s], bank[6 + s][:], ACT.Copy).then_inc(sems["y_taken"], 1)

            def experts(l):
                m = main[l]

                def step(e, s, first=False):
                    silu_of(m, s, e + 1)
                    if not first:
                        act.wait_ge(y_stored[l][1 - s], e * 8 - (16 - 8 * s))
                    take_y(m, 1 - s, e)

                silu_of(m, 0, 1)
                step(1, 1, first=True)
                step(2, 0, first=True)
                with act.Fori(0, EXPERTS // 2 - 2) as i:
                    for q in range(2):
                        step(i * 2 + (3 + q), 1 - q)
                act.wait_ge(y_stored[l][0], 8 * EXPERTS - 16)
                take_y(m, 0, EXPERTS - 1)
                silu_of(m, 1, EXPERTS)
                act.wait_ge(y_stored[l][1], 8 * EXPERTS - 16)
                take_y(m, 1, EXPERTS)
                n_over = act.value_load(ctl[0:1, 0:1], min_val=0, max_val=OVER)
                with act.If(n_over > 0):
                    act.wait_ge(y_stored[l][0], 16 * (EXPERTS // 2))
                    with act.Fori(0, n_over) as j:
                        silu_of(over[l], 0, j + 1)
                        take_y(over[l], 0, j + 1)
                for s in range(2):
                    act.wait_ge(y_stored[l][s], 16 * (EXPERTS // 2))
                act.wait_ge(moe_over, l + 1)
                for t in range(NT):
                    act.dma_start(y_in[t], y_dram[l][4 * t * P:4 * (t + 1) * P, :].rearrange("(p r) f -> p (r f)", r=4)
                                  ).then_inc(y_loaded[t], 16)

            route(0)
            act.wait_ge(lists_done, 1)
            experts(0)

            for t in range(NT):
                norm_stats(N_PRE[1], t)
                normalise(N_PRE[1], t)
            act.wait_ge(lam_sum, 1)
            a.activation(lam_t[:, 2:4], lam_t[:, 0:2], ACT.Exp).then_inc(lam_exp, 1)

            def qk_square(h, c):
                act.wait_ge(qk_ready, 2 * h + c + 1)
                a.activation(qk_sqb[c], qk_bank[c][:], ACT.Square).then_inc(qk_sq, 1)
                if h >= 1:
                    act.wait_ge(qk_done, 2 * h - 1 + c)
                a.activation(qk_g_sb[c], qk_bank[c][:], ACT.Copy, scale=qk_g[:, c:c + 1]).then_inc(qk_scaled, 1)

            def take_v(h):
                act.wait_ge(v_ready, h + 1)
                if h >= 2:
                    act.wait_ge(o_ready, 4 * (h - 1))
                a.activation(vh[h % 2].rearrange("p b f -> p (b f)"), v_bank[:], ACT.Copy).then_inc(v_done, 1)

            def probabilities(i):
                h, b = pairs[i]
                W = P * (b + 1)
                act.wait_ge(m_done, i + 1)
                if i >= 3:
                    act.wait_ge(a_done, i - 2)
                for c in range(2):
                    a.activation(p_sb[i % 3][:, c, 0:W], score[:, c, 0:W], ACT.Exp, bias=mx[:, i, c:c + 1],
                                 accum_out=ps[:, i, c:c + 1]).then_inc(p_done, 1)

            def o_squares(h):
                for b in range(NT):
                    i = NT * h + b
                    act.wait_ge(o_done, i + 1)
                    if i >= 1:
                        act.wait_ge(o_sq, i)
                    a.activation(o_junk, oh[h % 2][:, b, :], ACT.Square, accum_out=o_ssq[:, i:i + 1]).then_inc(o_sq, 1)

            def take_aT(i):
                b = pairs[i][1]
                act.wait_ge(aT_ready, i + 1)
                if i >= 2:
                    act.wait_ge(o_ready, i - 1)
                a.activation(aT[i % 2][:, 0:P * (b + 1)], aT_bank[:, 0:P * (b + 1)], ACT.Copy).then_inc(aT_done, 1)

            for h, g, e in attention_steps():
                if g is not None:
                    i = NT * g
                    take_v(g)
                    probabilities(i)
                    take_aT(i)
                    probabilities(i + 1)
                if h is not None:
                    qk_square(h, 0)
                if g is not None:
                    take_aT(i + 1)
                    probabilities(i + 2)
                if e is not None:
                    o_squares(e)
                if g is not None:
                    take_aT(i + 2)
                    probabilities(i + 3)
                if h is not None:
                    qk_square(h, 1)
                if g is not None:
                    take_aT(i + 3)
                if e is not None:
                    act.wait_ge(o_sq, NT * (e + 1))
                    cols = slice(NT * e, NT * (e + 1))
                    a.activation(o_std[:, cols], o_ssq[:, cols], ACT.Sqrt, bias=eps[:], scale=1.0 / P).then_inc(on_std, 1)
                if h is not None:
                    act.wait_ge(qk_ss, 2 * (h + 1))
                    a.activation(qk_std, ss_bank, ACT.Sqrt, bias=eps[:], scale=1.0 / HEAD_DIM).then_inc(qk_root, 1)

            route(1)
            act.wait_ge(lists_done, 2)
            experts(1)

        @block.vector
        def _(dve):
            v = nc.vector
            linked = [0]

            def link(ins):
                linked[0] += 1
                ins.then_inc(dve_chain, 1)
                dve.wait_ge(dve_chain, linked[0])

            def invert_rms(n, t):
                dve.wait_ge(std_done, 4 * n + t + 1)
                v.reciprocal(rstd[:, t:t + 1], std[:, t:t + 1]).then_inc(rstd_done, 1)

            def take_hT(n, t):
                for h in range(2):
                    dve.wait_ge(xt_ready, 8 * n + 2 * t + h + 1)
                    v.tensor_tensor(hT[:, 4 * h:4 * h + 4, t * P:(t + 1) * P],
                                    bank[6 + h][:].rearrange("p (j t) -> p j t", j=4),
                                    norm_g[:, n, 4 * h:4 * h + 4].unsqueeze(2).to_broadcast([P, 4, P]),
                                    ALU.mult).then_inc(xt_taken, 1)

            dve.wait_ge(consts_ready, 1)
            dve.wait_ge(gain_loaded, 16)
            for t in range(NT):
                invert_rms(N_PRE[0], t)
                if t >= 1:
                    take_hT(N_PRE[0], t - 1)
            take_hT(N_PRE[0], NT - 1)
            tap_count = [0]
            dve.wait_ge(chan_ready, 1)
            link(v.tensor_copy(chan[:], bank[5][:, 0:NC * (TAPS + 5)].rearrange("p (c r) -> p c r", c=NC)))
            v.memset(small_at(20), 0.0).then_inc(chan_taken, 1)

            def gated(ct):
                ub = u_buf[ct % 2]
                dve.wait_ge(gate_done, ct + 1)
                if ct >= 2:
                    dve.wait_ge(tap_made, (ct - 1) * POOL_TAPS)
                v.scalar_tensor_tensor(ub[:, PAD:PAD + T], bank[2 * (ct % 2)][:], chan[:, ct, TAPS + 3:TAPS + 4], sg[ct % 2],
                                       ALU.add, ALU.mult).then_inc(u_done, 1)

            gated(0)
            for ct in range(NC):
                ub = u_buf[ct % 2]
                dve.wait_ge(u_done, ct + 1)
                sums = (uT[:, ct, :], acc2)
                k0 = tap_count[0]
                for k, w in enumerate(range(POOL_TAPS, TAPS)):
                    acc = sums[k % 2]
                    if k >= 2:
                        dve.wait_ge(dve_taps, k0 + k - 1)
                    if k < 2:
                        ins = v.tensor_scalar(acc, ub[:, w:w + T], chan[:, ct, w:w + 1],
                                              chan[:, ct, TAPS:TAPS + 1] if k == 0 else 0.0, ALU.mult, ALU.add)
                    else:
                        ins = v.scalar_tensor_tensor(acc, ub[:, w:w + T], chan[:, ct, w:w + 1], acc, ALU.mult, ALU.add)
                    ins.then_inc(dve_taps, 1)
                tap_count[0] += TAPS - POOL_TAPS
                if ct + 1 < NC:
                    gated(ct + 1)
                dve.wait_ge(dve_taps, tap_count[0])
                link(v.tensor_tensor(uT[:, ct, :], uT[:, ct, :], acc2, ALU.add))
                dve.wait_ge(tap_added, (ct + 1) * (POOL_TAPS - 1))
                v.tensor_tensor(uT[:, ct, :], uT[:, ct, :], pacc[ct % 2], ALU.add).then_inc(conv_done, 1)
            dve.wait_ge(stats_ready, 1)
            link(v.tensor_scalar(ln_mu, bank[4][:], 1.0 / D, None, ALU.mult))
            link(v.tensor_tensor(ln_t, ln_mu, ln_mu, ALU.mult))
            link(v.scalar_tensor_tensor(ln_t, bank[5][:], 1.0 / D, ln_t, ALU.mult, ALU.subtract))
            v.tensor_scalar(ln_t, ln_t, 0.0, None, ALU.max).then_inc(ln_var, 1)
            dve.wait_ge(ln_std, 1)
            link(v.reciprocal(ln_r, ln_r))
            for ct in range(NC):
                link(v.tensor_tensor(uT[:, ct, :], uT[:, ct, :], ln_mu, ALU.subtract))
                v.tensor_tensor(uT[:, ct, :], uT[:, ct, :], ln_r, ALU.mult).then_inc(ln_x, 1)

            def add_mix(l):
                for t in range(NT):
                    for n in range(2):
                        k = 8 * l + 2 * t + n
                        dve.wait_ge(mix_ready, k + 1)
                        xs = x_res[:, t, n * 512:(n + 1) * 512]
                        ins = v.tensor_tensor(xs, xs, mix_bank(l, 2 * t + n)[:], ALU.add)
                        if n == 0:
                            link(ins)
                            if t >= 1:
                                take_hT(N_MOE[l], t - 1)
                        else:
                            ins.then_inc(x_done, 1)
                    invert_rms(N_MOE[l], t)
                take_hT(N_MOE[l], NT - 1)

            def route(l):
                bt = lambda ap, k: ap.unsqueeze(2).to_broadcast([P, ap.shape[1], k])
                dve.wait_ge(logits_ready, l + 1)
                logit = logit_bank[l][:, 0:NT * ROUTES].rearrange("p (t r) -> p t r", t=NT)
                link(v.tensor_copy(lg_g, logit[:, :, 0:GROUPS]))
                link(v.tensor_copy(lg_e.rearrange("p (t e) -> p t e", t=NT), logit[:, :, GROUPS:ROUTES]))
                iota_g = iota_exp[:, 0:GROUPS].unsqueeze(1).to_broadcast([P, NT, GROUPS])
                iota_e = iota_exp[:].unsqueeze(1).to_broadcast([P, NT, EXPERTS])
                index_g = iota_tile[:, 0:GROUPS].unsqueeze(1).to_broadcast([P, NT, GROUPS])
                index_e = iota_tile[:, 0:EXPERTS].unsqueeze(1).to_broadcast([P, NT, EXPERTS])
                link(v.tensor_reduce(v4(0), lg_g, AX.X, ALU.max))
                link(v.tensor_tensor(g_dif, lg_g, bt(v4(0), GROUPS), ALU.subtract))
                v.tensor_scalar(g_eq, g_dif, 0.0, None, ALU.is_ge).then_inc(exp_in, 1)
                dve.wait_ge(exp_in, 2 * l + 1)
                link(v.scalar_tensor_tensor(g_cand, g_eq, -99.0, index_g, ALU.mult, ALU.add))
                link(v.tensor_reduce(v4(1), g_cand, AX.X, ALU.min))
                link(v.tensor_tensor(g_eq, iota_g, bt(v4(1), GROUPS), ALU.is_equal))
                link(v.tensor_scalar(g_eq, g_eq, BIG, -BIG, ALU.mult, ALU.add))
                link(v.tensor_tensor(sel.rearrange("p t e -> p (t e)").rearrange("p (k e) -> p k e", e=PER_GROUP),
                                     lg_e.rearrange("p (k e) -> p k e", e=PER_GROUP),
                                     bt(g_eq.rearrange("p t g -> p (t g)"), PER_GROUP), ALU.add))
                for k in range(2):
                    top = v4(2) if k == 0 else v4(5)
                    link(v.tensor_reduce(top, sel, AX.X, ALU.max))
                    link(v.tensor_tensor(tmp, sel, bt(top, EXPERTS), ALU.is_ge))
                    link(v.scalar_tensor_tensor(tmp, tmp, -99.0, index_e, ALU.mult, ALU.add))
                    link(v.tensor_reduce(v8(0)[:, k * NT:(k + 1) * NT], tmp, AX.X, ALU.min))
                    link(v.tensor_tensor(pick[k], iota_e, bt(v8(0)[:, k * NT:(k + 1) * NT], EXPERTS), ALU.is_equal))
                    if k == 0:
                        link(v.scalar_tensor_tensor(sel, pick[0], -BIG, sel, ALU.mult, ALU.add))
                v.tensor_tensor(both, pick[0], pick[1], ALU.add).then_inc(picks_done, 1)
                v.tensor_tensor(v4(3), v4(5), v4(2), ALU.subtract).then_inc(exp_in, 1)
                dve.wait_ge(ranks_ready, l + 1)
                link(v.tensor_copy(rank, bank[4][:, 0:P].rearrange("p (t e) -> p t e", t=NT)))
                link(v.tensor_copy(count, bank[4][:, P:P + EXPERTS]))
                cmp_e = cmp.rearrange("p (e s) -> p e s", s=STEPS)
                link(v.tensor_tensor(cmp_e, bt(count, STEPS), steps[:].unsqueeze(1).to_broadcast([P, EXPERTS, STEPS]), ALU.is_gt))
                link(v.tensor_reduce(tiles_e, cmp_e, AX.X, ALU.add))
                link(v.tensor_tensor_scan(tiles_inc, ones[:, 0:EXPERTS], tiles_e, 0.0, ALU.mult, ALU.add))
                link(v.tensor_tensor(tiles_base, tiles_inc, tiles_e, ALU.subtract))
                two = lambda ap: ap.unsqueeze(1).to_broadcast([P, 2, NT * EXPERTS])
                eight = lambda ap: ap.rearrange("p (a e) -> p a e", e=EXPERTS)
                link(v.tensor_tensor(tmp2.rearrange("p (k n) -> p k n", k=2), picks.rearrange("p (k n) -> p k n", k=2),
                                     two(rank.rearrange("p t e -> p (t e)")), ALU.mult))
                link(v.tensor_reduce(v8(1), eight(tmp2), AX.X, ALU.add))
                link(v.tensor_tensor(eight(tmp2), eight(picks), tiles_base.unsqueeze(1).to_broadcast([P, 2 * NT, EXPERTS]), ALU.mult))
                link(v.tensor_reduce(v8(2), eight(tmp2), AX.X, ALU.add))
                cmp_a = cmp[:, 0:2 * NT * STEPS].rearrange("p (a s) -> p a s", s=STEPS)
                link(v.tensor_tensor(cmp_a, bt(v8(1), STEPS), steps[:].unsqueeze(1).to_broadcast([P, 2 * NT, STEPS]), ALU.is_ge))
                link(v.tensor_reduce(v8(3), cmp_a, AX.X, ALU.add))
                link(v.scalar_tensor_tensor(v8(4), v8(3), -float(SLOTS), v8(1), ALU.mult, ALU.add))
                link(v.tensor_scalar(v8(0), v8(0), 99.0, None, ALU.add))
                link(v.scalar_tensor_tensor(v8(5), v8(3), float(EXPERTS - 1), v8(2), ALU.add, ALU.add))
                link(v.tensor_tensor(v8(5), v8(5), v8(0), ALU.subtract))
                link(v.scalar_tensor_tensor(v8(5), v8(3), 0.0, v8(5), ALU.is_gt, ALU.mult))
                link(v.tensor_tensor(v8(5), v8(5), v8(0), ALU.add))
                link(v.tensor_tensor(hot_slot, iota_slot[:].unsqueeze(1).to_broadcast([P, 2 * NT, P]), bt(v8(4), P), ALU.is_equal))
                link(v.tensor_tensor(hot_tile, iota_tile[:].unsqueeze(1).to_broadcast([P, 2 * NT, TILES]), bt(v8(5), TILES), ALU.is_equal))
                v.tensor_tensor(hot_tile, hot_tile, bt(assign1[:].rearrange("p k t -> p (k t)"), TILES), ALU.mult).then_inc(hot_done, 1)
                oc = over_cmp[0:1, :].rearrange("p (j e) -> p j e", e=EXPERTS)
                link(v.tensor_tensor(oc, tiles_inc[0:1, :].unsqueeze(1).to_broadcast([1, OVER, EXPERTS]),
                                     iota_tile[0:1, 0:OVER].unsqueeze(2).to_broadcast([1, OVER, EXPERTS]), ALU.is_le))
                link(v.tensor_reduce(over_e[0:1, 1:OVER + 1], oc, AX.X, ALU.add))
                link(v.tensor_copy(over_e[0:1, 0:1], tiles_inc[0:1, EXPERTS - 1:EXPERTS]))
                link(v.tensor_scalar(ctl[:], over_e[0:1, :], float(EXPERTS), None, ALU.min))
                dve.wait_ge(exp_done, 2 * l + 1)
                link(v.tensor_reduce(v4(6), g_exp, AX.X, ALU.add))
                dve.wait_ge(exp_done, 2 * l + 2)
                link(v.tensor_scalar(v4(7), v4(4), 1.0, None, ALU.add))
                link(v.tensor_tensor(v4(6), v4(6), v4(7), ALU.mult))
                link(v.reciprocal(gates[:, 0, :], v4(6)))
                link(v.tensor_tensor(gates[:, 1, :], gates[:, 0, :], v4(4), ALU.mult))
                dve.wait_ge(lists_ready, l + 1)
                link(v.tensor_scalar(list_pad, bank[4][:, 256:256 + TILES], 0.0, FAR, ALU.is_equal, ALU.mult))
                link(v.tensor_scalar(list_f, bank[4][:, 256:256 + TILES], 2.0, half_m2[:], ALU.mult, ALU.add))
                link(v.tensor_tensor(rows_out[:], list_f, list_pad, ALU.add))
                link(v.tensor_scalar(list_i, rows_out[:], 1, 0x7FFFFFFE, ALU.logical_shift_right, ALU.bitwise_and))
                link(v.tensor_scalar(list_j, rows_out[:], 1, None, ALU.bitwise_and))
                v.tensor_tensor(rows_in[:], list_i, list_j, ALU.bitwise_or).then_inc(lists_done, 1)

            def take_xT(l, sems, s, e1):
                n = N_MOE[l]
                dve.wait_ge(sems["xT_ready"], e1)
                v.tensor_tensor(xeT[s].rearrange("p j h k -> p (j h) k"),
                                bank[s][:].rearrange("p (c k) -> p c k", k=SLOTS),
                                gain_jh[n], ALU.mult).then_inc(sems["xT_taken"], 1)

            def hidden(sems, s, e1):
                dve.wait_ge(sems["silu_done"], e1)
                v.tensor_tensor(h_sb[s], s_sb[s][SLOTS:P, :], bank[2 + s][SLOTS:P, :], ALU.mult).then_inc(sems["h_done"], 1)

            def take_hid(sems, s, e1):
                dve.wait_ge(sems["hid_ready"], e1)
                v.tensor_copy(hidT[s].rearrange("p j k -> p (j k)"), bank[4 + s][:, 0:256]).then_inc(sems["hid_taken"], 1)

            gain_jh = {}
            for l in range(LAYERS):
                n = N_MOE[l]
                g8 = gain_sb[:, l, :]
                gain_jh[n] = g8.unsqueeze(2).to_broadcast([P, NC, SLOTS])

            def experts(l):
                m = main[l]

                def step(e, s):
                    take_hid(m, 1 - s, e)
                    take_xT(l, m, 1 - s, e + 2)
                    hidden(m, s, e + 1)

                take_xT(l, m, 0, 1)
                take_xT(l, m, 1, 2)
                hidden(m, 0, 1)
                with dve.Fori(0, EXPERTS // 2 - 1) as i:
                    for q in range(2):
                        step(i * 2 + (1 + q), 1 - q)
                take_hid(m, 0, EXPERTS - 1)
                hidden(m, 1, EXPERTS)
                take_hid(m, 1, EXPERTS)
                n_over = dve.value_load(ctl[0:1, 0:1], min_val=0, max_val=OVER)
                with dve.If(n_over > 0):
                    with dve.Fori(0, n_over) as j:
                        take_xT(l, over[l], 0, j + 1)
                        hidden(over[l], 0, j + 1)
                        take_hid(over[l], 0, j + 1)
                for t in range(NT):
                    dve.wait_ge(y_loaded[t], 16 * (l + 1))
                    for k in range(2):
                        ins = v.scalar_tensor_tensor(x_res[:, t, :], y_in[t][:, k * D:(k + 1) * D], gates[:, k, t:t + 1],
                                                     x_res[:, t, :], ALU.mult, ALU.add)
                        if k == 0:
                            link(ins)
                            if l + 1 < LAYERS and t >= 1:
                                invert_rms(N_PRE[l + 1], t - 1)
                        else:
                            ins.then_inc(x_done, 1)
                    if l + 1 < LAYERS and t >= 2:
                        take_hT(N_PRE[l + 1], t - 2)

            dve.wait_ge(route_loaded, ROUTE_LOADS)
            for l in range(LAYERS):
                link(v.tensor_copy(gain_sb[:, l, :].rearrange("p (j h) -> p j h", h=2),
                                   norm_g[:, 2 * l + 1, :].rearrange("p (h j) -> p j h", h=2)))
            add_mix(0)
            route(0)
            experts(0)
            invert_rms(N_PRE[1], NT - 1)
            take_hT(N_PRE[1], NT - 2)
            take_hT(N_PRE[1], NT - 1)

            link(v.tensor_scalar(qk_g[:, 0:1], qk_g[:, 0:1], HEAD_DIM ** -0.5, None, ALU.mult))
            link(v.tensor_scalar(sub_g[:], sub_g[:], 1.0 - LAMBDA_INIT, None, ALU.mult))
            for c in range(2):
                link(v.tensor_tensor(lam_in[:, 2 * c, :], lam_in[:, 2 * c, :], lam_in[:, 2 * c + 1, :], ALU.mult))
                ins = v.tensor_reduce(lam_t[:, c:c + 1], lam_in[:, 2 * c, :], AX.X, ALU.add)
                if c == 0:
                    link(ins)
                else:
                    ins.then_inc(lam_sum, 1)
            dve.wait_ge(lam_exp, 1)
            link(v.tensor_tensor(neg_lam, lam_t[:, 3:4], lam_t[:, 2:3], ALU.subtract))
            link(v.tensor_scalar(neg_lam, neg_lam, -LAMBDA_INIT, None, ALU.add))

            def maxima(i):
                W = P * (pairs[i][1] + 1)
                dve.wait_ge(s_ready, i + 1)
                v.tensor_reduce(mx[:, i, :], score[:, :, 0:W], AX.X, ALU.max, negate=True).then_inc(m_done, 1)

            def combine(i):
                W = P * (pairs[i][1] + 1)
                dve.wait_ge(p_done, 2 * i + 2)
                v.reciprocal(o_r[:, i:i + 1], ps[:, i, 0:1])
                link(v.reciprocal(r1c[:, i:i + 1], ps[:, i, 1:2]))
                link(v.tensor_scalar(r1c[:, i:i + 1], ps[:, i, 0:1], r1c[:, i:i + 1], neg_lam, ALU.mult, ALU.mult))
                if i >= 2:
                    dve.wait_ge(aT_ready, i - 1)
                v.scalar_tensor_tensor(a_sb[i % 2][:, 0:W], p_sb[i % 3][:, 1, 0:W], r1c[:, i:i + 1],
                                       p_sb[i % 3][:, 0, 0:W], ALU.mult, ALU.add).then_inc(a_done, 1)

            def take_o(i):
                h, b = pairs[i]
                dve.wait_ge(o_ready, i + 1)
                v.tensor_scalar(oh[h % 2][:, b, :], o_bank[:, 0:P], o_r[:, i:i + 1], None, ALU.mult).then_inc(o_done, 1)

            def norm_qk(h, c):
                dve.wait_ge(qk_rs_ready, 2 * h + c + 1)
                v.tensor_tensor((qT, kT)[c][h % 2], qk_g_sb[c], rs_bank[c][:], ALU.mult).then_inc(qk_done, 1)

            for h, g, e in attention_steps():
                if g is not None:
                    i = NT * g
                    maxima(i)
                    combine(i)
                    maxima(i + 1)
                    combine(i + 1)
                    take_o(i)
                    maxima(i + 2)
                    combine(i + 2)
                    take_o(i + 1)
                    maxima(i + 3)
                    combine(i + 3)
                    take_o(i + 2)
                if h is not None:
                    dve.wait_ge(qk_root, h + 1)
                    link(v.reciprocal(qk_rs, qk_std))
                    for c in range(2):
                        v.tensor_copy(qk_rs_wide[c].rearrange("p (k f) -> p k f", f=HEAD_DIM),
                                      qk_rs[:, 2 * NT * c:2 * NT * (c + 1)].unsqueeze(2).to_broadcast([P, 2 * NT, HEAD_DIM])
                                      ).then_inc(qk_rec, 1)
                if e is not None:
                    dve.wait_ge(on_std, e + 1)
                    cols = slice(NT * e, NT * (e + 1))
                    link(v.reciprocal(o_rn[:, cols], o_std[:, cols]))
                    v.tensor_tensor(oh[e % 2], oh[e % 2], o_rn[:, cols].unsqueeze(2).to_broadcast([P, NT, P]),
                                    ALU.mult).then_inc(on_done, 1)
                if h is not None:
                    norm_qk(h, 0)
                if g is not None:
                    take_o(i + 3)
                if h is not None:
                    norm_qk(h, 1)
                if e is not None:
                    dve.wait_ge(oT_ready, e + 1)
                    v.tensor_scalar(oT[:, e, :], aT_bank[:], sub_g[:], None, ALU.mult).then_inc(oT_done, 1)
            add_mix(1)
            route(1)
            experts(1)

        @block.tensor
        def _(pe):
            mm = nc.tensor.matmul

            def transpose_xn(n, t):
                pe.wait_ge(xn_done, 4 * n + t + 1)
                for h in range(2):
                    m = 8 * n + 2 * t + h
                    if m >= 2:
                        pe.wait_ge(xt_taken, m - 1)
                    for j in range(4):
                        last = nc.tensor.transpose(bank[6 + h][:, j * P:(j + 1) * P],
                                                   xn[:, t, h * 512 + j:h * 512 + j + 509:4], ident[:])
                    last.then_inc(xt_ready, 1)

            def stay_warm(n, dst):
                for _ in range(n):
                    mm(dst[:], ident[:], x_res[:, 0, 0:512], start=True, stop=True)

            def project(dst, w, src, cols, start=True, stop=True):
                for c in range(NC):
                    last = mm(dst, w[:, c, cols], src[:, c, :], start=start and c == 0, stop=stop and c == NC - 1)
                return last

            pe.wait_ge(consts_ready, 1)
            for t in range(NT):
                transpose_xn(N_PRE[0], t)
            pe.wait_ge(params_loaded, 16 * 6)
            R = TAPS + 5
            for ct in range(NC):
                last = nc.tensor.transpose(bank[5][:, ct * R:(ct + 1) * R], chan_rows[:, ct * P:(ct + 1) * P], ident[0:R, 0:R])
            last.then_inc(chan_ready, 1)

            def stats(ct):
                pe.wait_ge(sq_done, ct + 1)
                mm(bank[4][:], ones[:], uT[:, ct, :], start=ct == 0, stop=ct == NC - 1)
                return mm(bank[5][:], ones[:], sq_ct[:, ct, :], start=ct == 0, stop=ct == NC - 1)

            pe.wait_ge(xt_taken, 8)
            pe.wait_ge(chan_taken, 1)
            for ct in range(NC):
                ua, ug = (0, 1) if ct < 4 else (2, 3)
                loaded(pe, ua)
                loaded(pe, ug)
                if ct >= 2:
                    pe.wait_ge(u_done, ct - 1)
                cols = slice((ct % 4) * P, (ct % 4 + 1) * P)
                project(bank[2 * (ct % 2)][:], w_chunks(ua), hT, cols)
                last = project(bank[2 * (ct % 2) + 1][:], w_chunks(ug), hT, cols)
                last.then_inc(glu_ready, 1)
                if ct >= 3:
                    stats(ct - 3)
            stats(NC - 3)
            stats(NC - 2)
            stats(NC - 1).then_inc(stats_ready, 1)

            def mix_out(l, n0, src, bias):
                for n in range(2):
                    loaded(pe, n0 + n)
                for t in range(NT):
                    for n in range(2):
                        k = 8 * l + 2 * t + n
                        dst = mix_bank(l, 2 * t + n)
                        if t >= 2:
                            pe.wait_ge(x_done, 8 * l + t - 1)
                        for c in range(NC - 1 if 2 * t + n < ahead[l] else 0, NC):
                            if t == 0 and n == 0:
                                pe.wait_ge((ln_done, oT_done)[l], c + 1)
                            last = mm(dst[:], src[:, c, t * P:(t + 1) * P], w_chunks(n0 + n)[:, c, :],
                                      start=c == 0, stop=c == NC - 1 and not bias)
                        if bias:
                            last = mm(dst[:], ones[0:1, :], b_out[:, n * 512:(n + 1) * 512], start=False, stop=True)
                        last.then_inc(mix_ready, 1)
                        if t >= 1 and n == 0:
                            transpose_xn(N_MOE[l], t - 1)
                        if t >= 1 and n == 1:
                            logits(l, t - 1)
                transpose_xn(N_MOE[l], NT - 1)
                logits(l, NT - 1)

            def logits(l, t):
                if l == 0 and t == 0:
                    pe.wait_ge(route_loaded, ROUTE_LOADS)
                dst = logit_bank[l][:, t * ROUTES:(t + 1) * ROUTES]
                pe.wait_ge(xt_taken, 8 * N_MOE[l] + 2 * t + 2)
                for c in range(NC):
                    mm(dst, hT[:, c, t * P:(t + 1) * P], w_route[:, l, c, :], start=c == 0, stop=False)
                last = mm(dst, ones[0:1, :], b_route[:, l, :], start=False, stop=True)
                if t == NT - 1:
                    last.then_inc(logits_ready, 1)

            def route(l):
                pe.wait_ge(picks_done, l + 1)
                for t in range(NT):
                    for u in range(t + 1):
                        mm(bank[4][:, t * EXPERTS:(t + 1) * EXPERTS], ones16[:] if u < t else before16[:], both[:, u, :],
                           start=u == 0, stop=u == t)
                for u in range(NT):
                    last = mm(bank[4][:, P:P + EXPERTS], ones16[:], both[:, u, :], start=u == 0, stop=u == NT - 1)
                last.then_inc(ranks_ready, 1)
                pe.wait_ge(hot_done, l + 1)
                for a in range(2 * NT):
                    last = mm(bank[4][:, 256:256 + TILES], hot_slot[:, a, :], hot_tile[:, a, :], start=a == 0, stop=a == 2 * NT - 1)
                last.then_inc(lists_ready, 1)
                stay_warm(4, bank[7])

            def rows_T(sems, s):
                for j in range(4):
                    last = nc.tensor.transpose(bank[s][:, j * P:(j + 1) * P], xe[s][:, j:j + 509:4], ident[:])
                last.then_inc(sems["xT_ready"], 1)

            def up(sems, s, w1, w3, e1):
                pe.wait_ge(sems["xT_taken"], e1)
                w1c, w3c = (w.rearrange("p (c n) -> p c n", c=NC) for w in (w1, w3))
                for h in range(2):
                    for j in range(4):
                        c = 4 * h + j
                        for q, w in ((0, w1c), (1, w3c)):
                            last = mm(bank[2 + s][q * SLOTS:(q + 1) * SLOTS, :], xeT[s][:, j, h, :], w[:, c, :],
                                      start=c == 0, stop=c == NC - 1)
                return last

            def hid_T(sems, s, e1):
                pe.wait_ge(sems["h_done"], e1)
                alone(pe)
                for j in range(4):
                    last = nc.tensor.transpose(bank[4 + s][:, j * SLOTS:(j + 1) * SLOTS], h_sb[s][:, j:j + 509:4],
                                               ident[0:SLOTS, 0:SLOTS])
                last.then_inc(sems["hid_ready"], 1)

            def down(sems, s, w2, e1):
                pe.wait_ge(sems["hid_taken"], e1)
                w2c = w2.rearrange("p (j n) -> p j n", j=4)
                for j in range(4):
                    for q in range(2):
                        last = mm(bank[6 + s][q * SLOTS:(q + 1) * SLOTS, :], hidT[s][:, j, :], w2c[:, j, q * 512:(q + 1) * 512],
                                  start=j == 0, stop=j == 3)
                return last

            def experts(l):
                m = main[l]
                n0 = FIRST[l] + MIX_UNITS[l]

                def up_step(e, s, weights):
                    (w1, *w1_loaded), (w3, *w3_loaded), _ = weights
                    pe.wait_ge(*w1_loaded)
                    pe.wait_ge(*w3_loaded)
                    up(m, s, w1, w3, e + 1).then_inc(m["up_ready"], 1)

                def rows_step(e, s):
                    pe.wait_ge(xe_loaded[l][s], e * 8 + (16 - 8 * s))
                    rows_T(m, s)

                def down_step(e, s, weights, first=False):
                    w2, *w2_loaded = weights[2]
                    pe.wait_ge(*w2_loaded)
                    if not first:
                        pe.wait_ge(m["y_taken"], e - 1)
                    down(m, s, w2, e + 1).then_inc(m["y_ready"], 1)

                def step(e, s, weights, before, first=False):
                    up_step(e, s, weights)
                    hid_T(m, 1 - s, e)
                    rows_step(e + 1, 1 - s)
                    down_step(e - 1, 1 - s, before, first)

                def in_ring(place, i=0):
                    units = [n0 + 3 * place + k for k in range(3)]
                    return [(unit(n), unit_loaded[n % RING], i * 32 + 32 * (n // RING + 1)) for n in units]

                extra = [(extra_units[k], extra_loaded[k], 32 * (l + 1)) for k in range(3)]
                rows_step(0, 0)
                rows_step(1, 1)
                up_step(0, 0, in_ring(0))
                step(1, 1, in_ring(1), in_ring(0), first=True)
                step(2, 0, extra, in_ring(1), first=True)
                third = in_ring(2)
                third[2] = (ahead_unit, *third[2][1:])
                step(3, 1, third, extra)
                step(4, 0, in_ring(3), third)
                step(5, 1, in_ring(4), in_ring(3))
                with pe.Fori(0, EXPERTS // 2 - 4) as i:
                    for q in range(2):
                        step(i * 2 + (6 + q), q, in_ring(5 + q, i), in_ring(4 + q, i))
                step(EXPERTS - 2, 0, in_ring(EXPERTS - 3), in_ring(EXPERTS - 4))
                hid_T(m, 0, EXPERTS - 1)
                down_step(EXPERTS - 2, 0, in_ring(EXPERTS - 3))
                up_step(EXPERTS - 1, 1, in_ring(EXPERTS - 2))
                hid_T(m, 1, EXPERTS)
                down_step(EXPERTS - 1, 1, in_ring(EXPERTS - 2))
                n_over = pe.value_load(ctl[0:1, 0:1], min_val=0, max_val=OVER)
                n1 = n0 + MOE_UNITS
                with pe.If(n_over > 0):
                    with pe.Fori(0, n_over) as j:
                        o = over[l]
                        pe.wait_ge(over_xe[l], j * 16 + 16)
                        rows_T(o, 0)
                        pe.wait_ge(over_w[l], j * 64 + 64)
                        up(o, 0, unit(n1), unit(n1 + 1), j + 1).then_inc(o["up_ready"], 1)
                        hid_T(o, 0, j + 1)
                        pe.wait_ge(over_w2[l], j * 32 + 32)
                        down(o, 0, unit(n1 + 2), j + 1).then_inc(o["y_ready"], 1)

            mix_out(0, 4, uT, True)
            route(0)
            pe.wait_ge(lists_done, 1)
            experts(0)

            for t in range(NT):
                transpose_xn(N_PRE[1], t)
            n0 = FIRST[1]
            pe.wait_ge(xt_taken, 8 * (N_PRE[1] + 1))

            def qk_half(h, c, half):
                u = n0 + 3 * (h // 4) + c
                if half == 0:
                    loaded(pe, u)
                    if h >= 1:
                        pe.wait_ge(qk_scaled, 2 * h - 1 + c)
                for k in range(4 * half, 4 * half + 4):
                    last = mm(qk_bank[c][:], w_chunks(u)[:, k, (h % 4) * P:(h % 4 + 1) * P], hT[:, k, :], start=k == 0, stop=k == NC - 1)
                if half == 1:
                    last.then_inc(qk_ready, 1)

            def sum_squares(h, c):
                pe.wait_ge(qk_sq, 2 * h + c + 1)
                if c == 0 and h >= 1:
                    pe.wait_ge(qk_done, 2 * h - 1)
                for t in range(NT):
                    k = 2 * (NT * c + t)
                    last = mm(ss_bank[:, k:k + 2], qk_sqb[c][:, t * P:(t + 1) * P], halves[:, 0:HEAD_DIM + 1:HEAD_DIM],
                              start=True, stop=True)
                last.then_inc(qk_ss, 1)

            def spread_rs(h, c):
                pe.wait_ge(qk_rec, 2 * h + c + 1)
                if c == 1 and h >= 1:
                    pe.wait_ge(p_done, 2 * NT * h)
                for t in range(NT):
                    last = mm(rs_bank[c][:, t * P:(t + 1) * P], qk_rs_wide[c][:, t * P:(t + 1) * P], ident[:], start=True, stop=True)
                last.then_inc(qk_rs_ready, 1)

            def v_half(h, half):
                u = n0 + 3 * (h // 4) + 2
                if half == 0:
                    loaded(pe, u)
                    if h >= 1:
                        pe.wait_ge(v_done, h)
                for t in (2 * half, 2 * half + 1):
                    for k in range(NC):
                        last = mm(v_bank[:, t * P:(t + 1) * P], hT[:, k, t * P:(t + 1) * P],
                                  w_chunks(u)[:, k, (h % 4) * P:(h % 4 + 1) * P], start=k == 0, stop=k == NC - 1)
                if half == 1:
                    last.then_inc(v_ready, 1)

            def scores(i):
                h, b = pairs[i]
                W = P * (b + 1)
                if b == 0:
                    pe.wait_ge(qk_done, 2 * (h + 1))
                if i >= 1:
                    pe.wait_ge(p_done, 2 * i)
                for c in range(2):
                    lo, hi = c * HEAD_DIM, (c + 1) * HEAD_DIM
                    mm(score[:, c, 0:W], qT[h % 2][lo:hi, b * P:(b + 1) * P], kT[h % 2][lo:hi, 0:W], start=True, stop=False,
                       skip_group_check=True)
                for c in range(2):
                    last = mm(score[:, c, W - CHUNK:W], mask_row[:], mask_col[:], start=False, stop=True,
                              skip_group_check=True)
                last.then_inc(s_ready, 1)

            def transposed(i):
                h, b = pairs[i]
                pe.wait_ge(a_done, i + 1)
                if i >= 1:
                    pe.wait_ge(aT_done, i)
                if b == 0 and h >= 2:
                    pe.wait_ge(oT_done, h - 1)
                for k in range(b + 1):
                    last = nc.tensor.transpose(aT_bank[:, k * P:(k + 1) * P], a_sb[i % 2][:, k * P:(k + 1) * P], ident[:])
                last.then_inc(aT_ready, 1)

            def weighted(i):
                h, b = pairs[i]
                pe.wait_ge(aT_done, i + 1)
                if b == 0:
                    pe.wait_ge(v_done, h + 1)
                if i >= 1:
                    pe.wait_ge(o_done, i)
                for k in range(b + 1):
                    last = mm(o_bank[:, 0:P], aT[i % 2][:, k * P:(k + 1) * P], vh[h % 2][:, k, :], start=k == 0, stop=k == b)
                last.then_inc(o_ready, 1)

            def output_T(e):
                pe.wait_ge(on_done, e + 1)
                if e + 1 < HEADS:
                    pe.wait_ge(aT_done, NT * (e + 2))
                for b in range(NT):
                    last = nc.tensor.transpose(aT_bank[:, b * P:(b + 1) * P], oh[e % 2][:, b, :], ident[:])
                last.then_inc(oT_ready, 1)

            def output_ahead(c):
                if c == 0:
                    loaded(pe, n0 + 6)
                    loaded(pe, n0 + 7)
                    pe.wait_ge(v_done, HEADS)
                pe.wait_ge(oT_done, c + 1)
                for k in range(ahead[1]):
                    t, n = k // 2, k % 2
                    mm(mix_bank(1, k)[:], oT[:, c, t * P:(t + 1) * P], w_chunks(n0 + 6 + n)[:, c, :], start=c == 0, stop=False)

            for h, g, e in attention_steps():
                last_head = h is None and g is not None
                if g is not None:
                    i = NT * g
                    scores(i)
                if h is not None:
                    qk_half(h, 0, 0)
                if last_head:
                    output_ahead(0)
                if g is not None:
                    transposed(i)
                    scores(i + 1)
                if h is not None:
                    qk_half(h, 0, 1)
                if last_head:
                    output_ahead(1)
                if g is not None:
                    weighted(i)
                    transposed(i + 1)
                    scores(i + 2)
                if h is not None:
                    qk_half(h, 1, 0)
                    sum_squares(h, 0)
                if last_head:
                    output_ahead(2)
                if g is not None:
                    weighted(i + 1)
                    transposed(i + 2)
                    scores(i + 3)
                if h is not None:
                    qk_half(h, 1, 1)
                if last_head:
                    output_ahead(3)
                if g is not None:
                    weighted(i + 2)
                if last_head:
                    output_ahead(4)
                if g is not None:
                    transposed(i + 3)
                if h is not None:
                    sum_squares(h, 1)
                    v_half(h, 0)
                if h is not None:
                    spread_rs(h, 0)
                    spread_rs(h, 1)
                if last_head:
                    output_ahead(5)
                if g is not None:
                    weighted(i + 3)
                if g is None and e is not None:
                    output_ahead(HEADS - 2)
                if e is not None:
                    output_T(e)
                if h is not None:
                    v_half(h, 1)
            mix_out(1, n0 + 6, oT, False)
            route(1)
            pe.wait_ge(lists_done, 2)
            experts(1)


_INS = ["x", "norm1_g", "norm2_g", "conv_w_in", "conv_b_in", "conv_dw", "conv_dw_b", "conv_ln_g", "conv_ln_b",
        "conv_w_out", "conv_b_out", "attn_w_qkv", "attn_q_g", "attn_k_g", "attn_lq1", "attn_lk1", "attn_lq2", "attn_lk2",
        "attn_subln_g", "attn_w_o", "moe_w_grp", "moe_b_grp", "moe_w_exp", "moe_b_exp", "moe_w1", "moe_w3", "moe_w2"]


def kernel(**inputs):
    import numpy as np
    import concourse.bacc as bacc
    from concourse.bass_utils import run_bass_kernel_spmd

    nc = bacc.Bacc("TRN2", target_bir_lowering=False, num_devices=1)
    arrays, args = {}, []
    for name in _INS:
        a = np.ascontiguousarray(inputs[name])
        arrays[f"in_{name}"] = a
        args.append(nc.dram_tensor(f"in_{name}", a.shape, mybir.dt.from_np(a.dtype), kind="ExternalInput").ap())
    args.append(nc.dram_tensor("out_x", (1, T, D), F32, kind="ExternalOutput").ap())
    trunk(nc, *args)
    return run_bass_kernel_spmd(nc, [arrays], core_ids=[0]).results[0]["out_x"]
```
